# Optimizing a Trainium2 kernel written in Bass

```python
import math
import jax, jax.numpy as jnp
from jax import lax
import numpy as np

D_MODEL = 1024
BATCH = 1
SEQ = 512
DEPTH = 2
DEC_BATCH = 8
DEC_SEQ = 4
PAST_LEN = 1024
PAGE_SIZE = 128

R_HEADS = 4
R_DK = 128
R_DV = 256
R_CHUNK = 128
R_QK = R_HEADS * R_DK
R_V = R_HEADS * R_DV
M_HEADS = 8
M_DH = 64
M_W = M_HEADS * M_DH
M_BLOCK = 256
M_TOPK = 3
M_QBLOCK = 128
ROPE_THETA = 10000.0
D_FF = -(-8 * D_MODEL // (3 * 256)) * 256
IN_WIDTH = 2 * R_QK + 2 * R_V + 3 * M_W + 2 * D_MODEL
NORM_EPS = 1e-6

kernel_name = "hybrid_retention_moba_decoder_step"

def rms_norm(x, g):
    xf = x.astype(jnp.float32)
    y = xf * lax.rsqrt(jnp.mean(xf * xf, axis=-1, keepdims=True) + NORM_EPS)
    return (y * g.astype(jnp.float32)).astype(x.dtype)

def head_rms(o):
    return o * lax.rsqrt(jnp.mean(o * o, axis=-1, keepdims=True) + NORM_EPS)

def split_proj(proj):
    widths = (R_QK, R_QK, R_V, R_V, M_W, M_W, M_W, D_MODEL, D_MODEL)
    out, start = [], 0
    for w in widths:
        out.append(proj[..., start:start + w])
        start += w
    return out

def retnet_rotate(x, pos):
    angle = 1.0 / (10000.0 ** jnp.linspace(0.0, 1.0, R_DK // 2, dtype=jnp.float32))
    ang = jnp.repeat(pos.astype(jnp.float32)[:, None] * angle[None, :], 2, axis=-1)[:, None, :]
    xf = x.astype(jnp.float32)
    rot = jnp.stack((-xf[..., 1::2], xf[..., ::2]), axis=-1).reshape(xf.shape)
    return (xf * jnp.cos(ang) + rot * jnp.sin(ang)).astype(x.dtype)

def rope(x, pos):
    half = M_DH // 2
    inv = ROPE_THETA ** (-jnp.arange(half, dtype=jnp.float32) / half)
    ang = pos.astype(jnp.float32)[:, None] * inv[None, :]
    cos, sin = jnp.cos(ang)[:, None, :], jnp.sin(ang)[:, None, :]
    xf = x.astype(jnp.float32)
    x1, x2 = xf[..., :half], xf[..., half:]
    return jnp.concatenate([x1 * cos - x2 * sin, x2 * cos + x1 * sin], axis=-1).astype(x.dtype)

def retention_chunk(q, k, v, s_prev, log_gamma):
    L = q.shape[1]
    n = jnp.arange(L, dtype=jnp.float32)
    diff = n[:, None] - n[None, :]
    decay = jnp.where(diff >= 0, jnp.exp(log_gamma[:, None, None] * jnp.maximum(diff, 0.0)), 0.0)
    qf, kf, vf = q.astype(jnp.float32), k.astype(jnp.float32), v.astype(jnp.float32)
    inner = jnp.einsum('bihd,bjhd->bhij', qf, kf) * decay[None]
    o = jnp.einsum('bhij,bjhv->bihv', inner, vf)
    q_decay = jnp.exp(log_gamma[None, :] * (n[:, None] + 1.0))
    o = o + jnp.einsum('bihd,bhdv->bihv', qf * q_decay[None, :, :, None], s_prev)
    k_decay = jnp.exp(log_gamma[None, :] * (L - 1.0 - n[:, None]))
    s_new = (jnp.exp(log_gamma * L)[None, :, None, None] * s_prev
             + jnp.einsum('bjhd,bjhv->bhdv', kf * k_decay[None, :, :, None], vf))
    return o, s_new

def retention_prompt(q, k, v, log_gamma):
    B, S = q.shape[:2]
    nc = S // R_CHUNK

    def to_chunks(t):
        return t.reshape((B, nc, R_CHUNK) + t.shape[2:]).swapaxes(0, 1)

    def step(s, xs):
        qc, kc, vc = xs
        o, s = retention_chunk(qc, kc, vc, s, log_gamma)
        return s, o

    s0 = jnp.zeros((B, R_HEADS, R_DK, R_DV), jnp.float32)
    s_fin, o = lax.scan(step, s0, (to_chunks(q), to_chunks(k), to_chunks(v)))
    return o.swapaxes(0, 1).reshape(B, S, R_HEADS, R_DV), s_fin

def moba_select(q, means, n_full, k_sel):
    s = jnp.einsum('hqd,hnd->hqn', q.astype(jnp.float32), means.astype(jnp.float32))
    cand = jnp.arange(means.shape[1])[None, None, :] < n_full[None, :, None]
    s = jnp.where(cand, s, -jnp.inf)
    _, idx = lax.top_k(s, k_sel)
    valid = idx < n_full[None, :, None]
    return idx, valid

def moba_core(q, kg, vg, valid, k_own, v_own, own_mask):
    qf = q.astype(jnp.float32) * (M_DH ** -0.5)
    s_own = jnp.einsum('hqd,hkd->hqk', qf, k_own.astype(jnp.float32))
    s_own = jnp.where(own_mask[None], s_own, -jnp.inf)
    if kg is None:
        p = jax.nn.softmax(s_own, axis=-1)
        return jnp.einsum('hqk,hkd->hqd', p, v_own.astype(jnp.float32))
    H, Q, ks, blk = kg.shape[:4]
    s_past = jnp.einsum('hqd,hqnkd->hqnk', qf, kg.astype(jnp.float32))
    s_past = jnp.where(valid[..., None], s_past, -jnp.inf).reshape(H, Q, ks * blk)
    p = jax.nn.softmax(jnp.concatenate([s_past, s_own], axis=-1), axis=-1)
    p_past = p[..., :ks * blk].reshape(H, Q, ks, blk)
    p_own = p[..., ks * blk:]
    return (jnp.einsum('hqnk,hqnkd->hqd', p_past, vg.astype(jnp.float32))
            + jnp.einsum('hqk,hkd->hqd', p_own, v_own.astype(jnp.float32)))

def moba_prompt(q, k, v):
    B, S = q.shape[:2]
    nb_pad = -(-S // M_BLOCK)
    pad = nb_pad * M_BLOCK - S
    kp = jnp.pad(k, ((0, 0), (0, pad), (0, 0), (0, 0)))
    vp = jnp.pad(v, ((0, 0), (0, pad), (0, 0), (0, 0)))
    kb = kp.reshape(B, nb_pad, M_BLOCK, M_HEADS, M_DH).transpose(0, 3, 1, 2, 4)
    vb = vp.reshape(B, nb_pad, M_BLOCK, M_HEADS, M_DH).transpose(0, 3, 1, 2, 4)
    n_cand = (S - 1) // M_BLOCK
    k_sel = min(M_TOPK, n_cand)
    means = jnp.mean(kb[:, :, :n_cand].astype(jnp.float32), axis=3) if k_sel > 0 else None
    qh = q.transpose(0, 2, 1, 3)
    nq = S // M_QBLOCK

    def one(n):
        b = n // nq
        q0 = (n % nq) * M_QBLOCK
        q_blk = lax.dynamic_slice(qh, (b, 0, q0, 0), (1, M_HEADS, M_QBLOCK, M_DH))[0]
        kb_b = lax.dynamic_index_in_dim(kb, b, 0, keepdims=False)
        vb_b = lax.dynamic_index_in_dim(vb, b, 0, keepdims=False)
        pos = q0 + jnp.arange(M_QBLOCK)
        own = q0 // M_BLOCK
        k_own = lax.dynamic_index_in_dim(kb_b, own, 1, keepdims=False)
        v_own = lax.dynamic_index_in_dim(vb_b, own, 1, keepdims=False)
        own_mask = (own * M_BLOCK + jnp.arange(M_BLOCK))[None, :] <= pos[:, None]
        if k_sel > 0:
            m_b = lax.dynamic_index_in_dim(means, b, 0, keepdims=False)
            idx, valid = moba_select(q_blk, m_b, pos // M_BLOCK, k_sel)
            kg = jax.vmap(lambda t, i: t[i])(kb_b, idx)
            vg = jax.vmap(lambda t, i: t[i])(vb_b, idx)
        else:
            kg = vg = valid = None
        return moba_core(q_blk, kg, vg, valid, k_own, v_own, own_mask)

    out = lax.map(one, jnp.arange(B * nq))
    out = out.reshape(B, nq, M_HEADS, M_QBLOCK, M_DH).transpose(0, 1, 3, 2, 4).reshape(B, S, M_W)
    return out.astype(q.dtype)

def moba_sample(q, k_new, v_new, k_pages, v_pages, page_table):
    DB, L = q.shape[:2]
    n_pages = page_table.shape[1]
    past_len = n_pages * PAGE_SIZE
    ppb = M_BLOCK // PAGE_SIZE
    n_full = past_len // M_BLOCK
    k_sel = min(M_TOPK, n_full)
    tail_page0 = n_full * ppb
    tail_len = past_len - n_full * M_BLOCK
    pos = past_len + jnp.arange(L)
    own_pos = n_full * M_BLOCK + jnp.arange(tail_len + L)
    own_mask = own_pos[None, :] <= pos[:, None]
    n_full_q = pos // M_BLOCK
    hidx = jnp.arange(M_HEADS)[:, None, None, None]

    def one(q_b, kn_b, vn_b, pt_b):
        qh = q_b.swapaxes(0, 1)
        k_tail = k_pages[pt_b[tail_page0:]].reshape(tail_len, M_HEADS, M_DH)
        v_tail = v_pages[pt_b[tail_page0:]].reshape(tail_len, M_HEADS, M_DH)
        k_own = jnp.concatenate([k_tail.astype(jnp.float32), kn_b.astype(jnp.float32)], 0).swapaxes(0, 1)
        v_own = jnp.concatenate([v_tail.astype(jnp.float32), vn_b.astype(jnp.float32)], 0).swapaxes(0, 1)
        if k_sel > 0:
            k_full = k_pages[pt_b[:n_full * ppb]].reshape(n_full, M_BLOCK, M_HEADS, M_DH)
            means = jnp.mean(k_full.astype(jnp.float32), axis=1).swapaxes(0, 1)
            idx, valid = moba_select(qh, means, n_full_q, k_sel)
            phys = pt_b[idx[..., None] * ppb + jnp.arange(ppb)]
            kg = k_pages[phys, :, hidx].reshape(M_HEADS, L, k_sel, M_BLOCK, M_DH)
            vg = v_pages[phys, :, hidx].reshape(M_HEADS, L, k_sel, M_BLOCK, M_DH)
        else:
            kg = vg = valid = None
        return moba_core(qh, kg, vg, valid, k_own, v_own, own_mask)

    out = jax.vmap(one)(q, k_new, v_new, page_table)
    return out.swapaxes(1, 2).reshape(DB, L, M_W).astype(q.dtype)

def forward(x, pos, ret_mix, attn_mix, g_mix, w_in, w_br_ret, w_br_att, w_out, g_ffn, w_gu, w_down, g_final):
    B, L = x.shape[:2]
    states = []
    for l in range(DEPTH):
        h = rms_norm(x, g_mix[l])
        proj = jnp.einsum('bld,de->ble', h, w_in[l])
        rq, rk, rv, rg, mq, mk, mv, gate_r, gate_a = split_proj(proj)
        rq = retnet_rotate(rq.reshape(B, L, R_HEADS, R_DK), pos)
        rk = retnet_rotate(rk.reshape(B, L, R_HEADS, R_DK), pos) * (R_DK ** -0.5)
        rv = rv.reshape(B, L, R_HEADS, R_DV)
        ro, r_state = ret_mix(l, rq, rk, rv)
        ro = (head_rms(ro).reshape(B, L, R_V) * jax.nn.silu(rg.astype(jnp.float32))).astype(x.dtype)
        mq = rope(mq.reshape(B, L, M_HEADS, M_DH), pos)
        mk = rope(mk.reshape(B, L, M_HEADS, M_DH), pos)
        mv = mv.reshape(B, L, M_HEADS, M_DH)
        mo = attn_mix(l, mq, mk, mv)
        merged = (jax.nn.sigmoid(gate_r) * (ro @ w_br_ret[l])
                  + jax.nn.sigmoid(gate_a) * (mo @ w_br_att[l]))
        x = x + merged @ w_out[l]
        h2 = rms_norm(x, g_ffn[l])
        gu = h2 @ w_gu[l]
        x = x + (jax.nn.silu(gu[..., :D_FF]) * gu[..., D_FF:]) @ w_down[l]
        states.append((mk, mv, r_state))
    return rms_norm(x, g_final), states

def setup_inputs(seed: int = 0) -> dict:
    key = jax.random.key(seed)
    ks = jax.random.split(key, 18)
    f32 = jnp.float32
    n_pages = PAST_LEN // PAGE_SIZE
    n_pool = (DEC_BATCH * n_pages * 5) // 4

    def nrm(k, shape, scale):
        return jax.random.normal(k, shape, f32) * scale

    perm = jax.random.permutation(ks[5], n_pool)[: DEC_BATCH * n_pages]
    return {
        "x_prompt": nrm(ks[0], (BATCH, SEQ, D_MODEL), 1.0),
        "x_sample": nrm(ks[1], (DEC_BATCH, DEC_SEQ, D_MODEL), 1.0),
        "cache_k": nrm(ks[2], (DEPTH, n_pool, PAGE_SIZE, M_HEADS, M_DH), 1.0),
        "cache_v": nrm(ks[3], (DEPTH, n_pool, PAGE_SIZE, M_HEADS, M_DH), 1.0),
        "state_ret": nrm(ks[4], (DEPTH, DEC_BATCH, R_HEADS, R_DK, R_DV), 1.0),
        "page_table": perm.reshape(DEC_BATCH, n_pages).astype(jnp.int32),
        "g_mix": 1.0 + nrm(ks[6], (DEPTH, D_MODEL), 0.02),
        "w_in": nrm(ks[7], (DEPTH, D_MODEL, IN_WIDTH), D_MODEL ** -0.5),
        "w_br_ret": nrm(ks[8], (DEPTH, R_V, D_MODEL), R_V ** -0.5),
        "w_br_att": nrm(ks[9], (DEPTH, M_W, D_MODEL), M_W ** -0.5),
        "w_out": nrm(ks[10], (DEPTH, D_MODEL, D_MODEL), D_MODEL ** -0.5),
        "g_ffn": 1.0 + nrm(ks[11], (DEPTH, D_MODEL), 0.02),
        "w_gu": nrm(ks[12], (DEPTH, D_MODEL, 2 * D_FF), D_MODEL ** -0.5),
        "w_down": nrm(ks[13], (DEPTH, D_FF, D_MODEL), D_FF ** -0.5),
        "g_final": 1.0 + nrm(ks[14], (D_MODEL,), 0.02),
    }

def reference(x_prompt, x_sample, cache_k, cache_v, state_ret, page_table,
              g_mix, w_in, w_br_ret, w_br_att, w_out, g_ffn, w_gu, w_down, g_final):
    weights = (g_mix, w_in, w_br_ret, w_br_att, w_out, g_ffn, w_gu, w_down, g_final)
    log_gamma = jnp.log1p(-jnp.exp2(-5.0 - jnp.arange(R_HEADS, dtype=jnp.float32)))

    pos_p = jnp.arange(x_prompt.shape[1])

    def ret_prompt(l, q, k, v):
        return retention_prompt(q, k, v, log_gamma)

    def att_prompt(l, q, k, v):
        return moba_prompt(q, k, v)

    y_prompt, st_p = forward(x_prompt, pos_p, ret_prompt, att_prompt, *weights)

    past_len = page_table.shape[1] * PAGE_SIZE
    pos_s = past_len + jnp.arange(x_sample.shape[1])

    def ret_sample(l, q, k, v):
        return retention_chunk(q, k, v, state_ret[l].astype(jnp.float32), log_gamma)

    def att_sample(l, q, k, v):
        return moba_sample(q, k, v, cache_k[l], cache_v[l], page_table)

    y_sample, st_s = forward(x_sample, pos_s, ret_sample, att_sample, *weights)

    k_prompt = jnp.stack([s[0] for s in st_p])
    v_prompt = jnp.stack([s[1] for s in st_p])
    state_ret_prompt = jnp.stack([s[2] for s in st_p]).astype(state_ret.dtype)
    k_sample = jnp.stack([s[0] for s in st_s])
    v_sample = jnp.stack([s[1] for s in st_s])
    state_ret_sample = jnp.stack([s[2] for s in st_s]).astype(state_ret.dtype)
    return (y_prompt, y_sample, k_prompt, v_prompt, state_ret_prompt, k_sample, v_sample, state_ret_sample)


_drawn_inputs = setup_inputs


def setup_inputs(seed=0):
    import zlib

    import numpy as np

    out = dict(_drawn_inputs(seed))
    spreads = {}
    factors = {'g_ffn': 2.758, 'g_final': 2.861}
    for name, (base, spread) in spreads.items():
        noise = np.random.default_rng([zlib.crc32(name.encode()), seed]).standard_normal(out[name].shape)
        drawn = base * np.exp(spread * noise) if base else spread * noise
        out[name] = __import__('jax').numpy.asarray(drawn.astype(out[name].dtype))
    for name, factor in factors.items():
        out[name] = (out[name] * factor).astype(out[name].dtype)
    return out
```

```python
from contextlib import ExitStack, contextmanager

import numpy as np

import concourse.bass as bass
from concourse import mybir

F32 = mybir.dt.float32
F32R = mybir.dt.float32r
I32 = mybir.dt.int32
ALU = mybir.AluOpType
ACT = mybir.ActivationFunctionType
AX = mybir.AxisListType.X

P = 128
D_MODEL, SEQ, DEPTH = 1024, 512, 2
DEC_B, DEC_L, PAST, PAGE = 8, 4, 1024, 128
R_HEADS, R_DK, R_DV = 4, 128, 256
M_HEADS, M_DH, M_BLOCK = 8, 64, 256
D_FF = 2816
EPS = 1e-6
NS = DEC_B * DEC_L
N = SEQ + NS
HALF = N // 2
KT = D_MODEL // P
FT = D_FF // P
TT = SEQ // P + 1
ROWS = [P] * (TT - 1) + [NS]
UC = 256
N_PAGES = PAST // PAGE
GRP = 4
NG = DEC_B // GRP
BIG = 1e30
M_SCALE = M_DH ** -0.5
LOG_G = np.log1p(-np.exp2(-5.0 - np.arange(R_HEADS, dtype=np.float32))).astype(np.float32)
G_CHUNK = [float(x) for x in np.exp(LOG_G * np.float32(P))]
G_STEP = [float(x) for x in np.exp(LOG_G * np.float32(DEC_L))]

PHASES = [("mqk", 4, 20), ("mv", 2, 10), ("rqk", 4, 20), ("rv", 4, 20), ("rg", 4, 8), ("br_ret", 8, 16),
          ("br_att", 8, 16), ("out", 4, 8), ("gu", 22, 44), ("down", 16, 8)]
U0, T0, _u, _t = {}, {}, 0, 1
for _n, _a, _b in PHASES:
    U0[_n], T0[_n] = _u, _t
    _u, _t = _u + _a, _t + _b
NU, NT = _u, _t - 1
NX = 4 * KT + FT
X0 = {"rg": KT, "br_att": 2 * KT, "out": 3 * KT, "gu": 4 * KT, "down": 4 * KT + FT}
S0N = {"rg": 0, "br_ret": KT, "br_att": 2 * KT, "gu": 3 * KT}
V0N = {"rg": 0, "br_att": KT, "gu": 2 * KT}
NSIG, NVAL = 3 * KT + FT, 2 * KT + FT
C_MQ, C_MV, C_RQ, C_RV, C_RG, C_GR, C_GA = 3072, 4096, 0, 1024, 2048, 4608, 5632

CA_PARTS = [("causal", P), ("dect", 4 * P), ("qdt", 4 * P), ("cosr", TT * 64), ("sinr", TT * 64),
            ("cosm", TT * 32), ("sinm", TT * 32), ("kdec", 4), ("kdecs", 4), ("own", NG * NS), ("headm", 8),
            ("sel", 16), ("seqm", 8), ("qds", 128), ("decs", 128), ("rank", 4)]
CA, _c = {}, 0
for _n, _w in CA_PARTS:
    CA[_n] = (_c, _w)
    _c += _w
NCA = _c


def shape_constants():
    f = np.float32
    t = np.zeros((P, NCA), f)

    def put(name, a):
        a = np.asarray(a, f)
        t[:a.shape[0], CA[name][0]:CA[name][0] + CA[name][1]] = a.reshape(a.shape[0], -1)

    pos = np.zeros((P, TT), f)
    for i in range(TT - 1):
        pos[:, i] = i * P + np.arange(P)
    pos[:NS, TT - 1] = PAST + np.arange(NS) % DEC_L
    fr = (f(1.0) / np.power(f(10000.0), np.linspace(0.0, 1.0, R_DK // 2, dtype=f))).astype(f)
    fm = np.power(f(10000.0), (-np.arange(32, dtype=f) / f(32))).astype(f)
    for fq, c, s in ((fr, "cosr", "sinr"), (fm, "cosm", "sinm")):
        a = (pos[:, :, None] * fq[None, None, :]).astype(f).astype(np.float64)
        put(c, np.cos(a))
        put(s, np.sin(a))
    i, j = np.arange(P)[None, :], np.arange(P)[:, None]
    put("causal", np.where(j >= i, 0.0, -BIG))
    lg = LOG_G
    diff = (i - j).astype(f)
    put("dect", np.stack([np.where(diff >= 0, np.exp(g * np.maximum(diff, 0)), 0) for g in lg], 1))
    put("qdt", np.broadcast_to(np.exp(lg[:, None] * (np.arange(P, dtype=f)[None] + 1))[None], (P, 4, P)))
    put("kdec", np.exp(lg[None, :] * (P - 1.0 - np.arange(P, dtype=f)[:, None])))
    b, q = np.arange(NS) // DEC_L, (np.arange(NS) % DEC_L).astype(f)
    put("kdecs", np.exp(lg[None, :] * (DEC_L - 1.0 - q[:, None])))
    put("qds", np.broadcast_to(np.exp(lg[:, None] * (q[None] + 1))[None], (P, 4, NS)))
    same = b[:, None] == b[None, :]
    ds = q[None, :] - q[:, None]
    put("decs", np.stack([np.where(same & (ds >= 0), np.exp(g * np.maximum(ds, 0)), 0) for g in lg], 1))
    put("seqm", b[:, None] == np.arange(DEC_B)[None])
    r = np.arange(P)
    rb, rh, rq = r // 32, (r % 32) // 4, r % 4
    put("own", np.stack([np.where((b[None] == (g * GRP + rb)[:, None]) & (q[None] <= rq[:, None]), 0.0, -BIG)
                         for g in range(NG)], 1))
    put("headm", rh[:, None] == np.arange(8)[None])
    put("sel", (rb * 4 + rq)[:, None] == np.arange(16)[None])
    put("rank", np.broadcast_to(np.arange(1, 5, dtype=f), (P, 4)))
    return t, np.concatenate([np.eye(P, dtype=f), np.ones((P, P), f)], 1)


class Order:

    def __init__(self, eng, sem):
        self.eng, self.sem, self.base, self.n = eng, sem, 0, 0

    def mark(self, ins):
        ins.then_inc(self.sem, 1)
        self.n += 1

    def wait(self):
        self.eng.wait_ge(self.sem, self.base + self.n)

    def hold(self):
        hold(self.eng, self.sem, self.base + self.n)

    @contextmanager
    def loop(self, count, each):
        base, n = self.base, self.n
        with self.eng.Fori(0, count) as i:
            self.base, self.n = base + n + i * each, 0
            yield i
            assert self.n == each, f"marks in the loop: {self.n}, not {each}"
        self.base, self.n = base, n + count * each


IDLE = []


def hold(eng, sem, value):
    if isinstance(value, int):
        return eng.wait_ge(sem, value)
    with eng.register() as count:
        eng.reg_mov(count, value)
        eng.wait_ge(IDLE[0], 0)
        eng.wait_ge(sem, count)


def build(nc, x_prompt, x_sample, cache_k, cache_v, state_ret, page_table, g_mix, w_in, w_br_ret, w_br_att,
          w_out, g_ffn, w_gu, w_down, g_final, consts_layer, consts_fixed,
          y_prompt, y_sample, k_prompt, v_prompt, state_prompt, k_sample, v_sample, state_sample):
    ctx = ExitStack()
    top = [16512]

    def at(name, shape, dt=F32, off=None):
        size = 4 * int(np.prod(shape[1:]))
        if off is None:
            off, top[0] = top[0], top[0] + (size + 31) // 32 * 32
        assert off + size <= 229344, (name, off + size)
        return nc.alloc_sbuf_tensor_at(name, shape, dt, offset=off)

    def sem(name):
        return ctx.enter_context(nc.semaphore(name))

    XT = at("XT", [P, KT, N])
    XH, XL = at("XH", [P, KT, N], F32R), at("XL", [P, KT, N], F32R)
    RAW = at("RAW", [P, 2, 8 * UC])
    WH, WL = at("WH", [P, 2, 8 * UC], F32R), at("WL", [P, 2, 8 * UC], F32R)
    FIX = at("FIX", [P, 2 * P])
    IDENT, ONES = FIX[:, 0:P], FIX[:, P:2 * P]
    GT = at("GT", [P, 40])
    RSTDB = at("RSTDB", [P, N])
    EA = at("EA", [P, 2, N])
    EB = at("EB", [P, 2, N])
    SM = at("SM", [P, 96])
    RT, RTK, VAR = SM[:, 0:5], SM[:, 5:10], SM[:, 10:15]
    MX, NM, RSUM, RINV = SM[:, 16:18], SM[:, 18:20], SM[:, 20:22], SM[:, 22:24]
    SSQ, RMS, RRS = SM[:, 24:28], SM[:, 28:32], SM[:, 32:36]
    BS, BM, PEN, BIAS, EQ = SM[:, 40:44], SM[:, 44:49], SM[:, 50:54], SM[:, 54:59], SM[:, 60:64]
    T1A, ES, SRI, MHALF = SM[:, 64:66], SM[:, 68:73], SM[:, 74:75], SM[:, 80:85]
    PTAB = at("PTAB", [1, DEC_B * N_PAGES], I32)
    XS = EA[:, 0, 0:512].rearrange("p (a c) -> p a c", a=2)
    RO1, RO2 = EA[:, 1, 0:256], EA[:, 1, 256:512]
    IND, QD = EA[:, 0, 0:512], EA[:, 1, 0:512]
    DIAG = EA[:].rearrange("p a n -> p (a n)")[:, 0:TT * P].rearrange("p (t c) -> p t c", t=TT)

    R0 = top[0]
    AH, AL = at("AH", [P, FT, N], F32R, R0), at("AL", [P, FT, N], F32R, R0 + FT * N * 4)
    CL = at("CL", [P, NCA], F32, R0)
    R1 = R0 + NCA * 4 + 32 & ~31
    MOH, MOL = at("MOH", [P, 4, N], F32R, R1), at("MOL", [P, 4, N], F32R, R1 + 16 * N)
    GREG = R1 + 32 * N
    G1 = at("G1", [P, KT, N], F32, GREG)
    ROREG = GREG + 4 * KT * N
    ROH, ROL = at("ROH", [P, KT, N], F32R, ROREG), at("ROL", [P, KT, N], F32R, ROREG + 4 * KT * N)
    o = GREG
    MT = at("MT", [P, 8, N], F32, o); o += 32 * N
    MV = at("MV", [P, TT, 512], F32, o); o += TT * 2048
    PG = at("PG", [P, 2, GRP, 512], F32, o); o += GRP * 4096
    QK = at("QK", [P, TT, 1024], F32, o)
    PR = at("PR", [P, 2, 512], F32, o)
    PT = at("PT", [P, 2, 4, 512], F32, o + 4096)
    KTT = at("KTT", [P, GRP, 4, P], F32, o); o += GRP * 2048
    SP_ = at("SP_", [P, PAST + NS], F32, o); o += 4 * (PAST + NS)
    PTS = at("PTS", [P, 9, P], F32, o); o += 9 * 512
    QB = at("QB", [P, 4, 256], F32, o); o += 4096
    OS = at("OS", [P, 512], F32, o)
    RQ = at("RQ", [P, TT, 512], F32, GREG)
    ROT = G1
    o = ROREG
    RTT = at("RTT", [P, 8, N], F32, o); o += 32 * N
    RK = at("RK", [P, TT, 512], F32, o)
    QM = at("QM", [P, 4, 256], F32, o)
    KM = at("KM", [P, 2, 512], F32, o + 4096); o += TT * 2048
    RV = at("RV", [P, TT, 1024], F32, o)
    S0 = at("S0", [P, 2, 4, 256], F32, o)
    SN = at("SN", [P, 2, 4, 256], F32, o + 8192); o += TT * 4096
    ST = at("ST", [P, 4, 256], F32, o)
    XIN = at("XIN", [P, TT, D_MODEL], F32, GREG)
    GIN = at("GIN", [40, P], F32, GREG + TT * 4096)
    YO = at("YO", [P, 2, D_MODEL], F32, GREG)

    PS = ctx.enter_context(nc.psum_tensor("PS", [P, 8, 512], F32))

    def cl(name, rows=P):
        a, w = CA[name]
        return CL[0:rows, a:a + w]

    IDLE[:] = [sem("idle")]
    consts_in, x_in, g_in, ptab_in = sem("consts_in"), sem("x_in"), sem("g_in"), sem("ptab_in")
    cl_in = sem("cl_in")
    landed = [sem("landed0"), sem("landed1")]
    hi_ready, lo_ready, half_done = sem("hi_ready"), sem("lo_ready"), sem("half_done")
    tile_done, tile_free = sem("tile_done"), sem("tile_free")
    rot_free = sem("rot_free")
    dve_own, act_own = sem("dve_own"), sem("act_own")
    xt_done, xt_copied, g_ready, x_lo = sem("xt_done"), sem("xt_copied"), sem("g_ready"), sem("x_lo")
    sq_added, nsum, nvar, nrt, ndiag, nbc = (sem(s) for s in ("sq_added", "nsum", "nvar", "nrt", "ndiag", "nbc"))
    xg_ready, mhalf_set = sem("xg_ready"), sem("mhalf_set")
    tr_done, tr_act, tr_dve = sem("tr_done"), sem("tr_act"), sem("tr_dve")
    s_done, s_max, s_exp, s_prob = sem("s_done"), sem("s_max"), sem("s_exp"), sem("s_prob")
    pt_done, pt_evac, pv_done, mo_hi, mo_lo = (sem(s) for s in ("pt_done", "pt_evac", "pv_done", "mo_hi", "mo_lo"))
    page_in = [sem("page_in0"), sem("page_in1")]
    qb_ready, kt_done, kt_act, kt_dve, sc_done = (sem(s) for s in ("qb_ready", "kt_done", "kt_act", "kt_dve", "sc_done"))
    sel_ready, e_done, pts_done, pts_act, pts_dve = (sem(s) for s in ("sel_ready", "e_done", "pts_done", "pts_act", "pts_dve"))
    pvs_page, os_ready, mos_done, mos_hi, mos_lo = (sem(s) for s in ("pvs_page", "os_ready", "mos_done", "mos_hi", "mos_lo"))
    kv_out, st_out, y_out = sem("kv_out"), sem("st_out"), sem("y_out")
    kd_ready, in_done, in_masked, o_done, st_done, st_ready = (
        sem(s) for s in ("kd_ready", "in_done", "in_masked", "o_done", "st_done", "st_ready"))
    ssq_ready, var_ready, rms_ready, o_scaled, ot_done, ot_act, ot_dve = (
        sem(s) for s in ("ssq_ready", "var_ready", "rms_ready", "o_scaled", "ot_done", "ot_act", "ot_dve"))
    s0_in = [sem("s0_in0"), sem("s0_in1")]
    sn_out = [sem("sn_out0"), sem("sn_out1")]
    qm_ready, km_ready, ss_done, sn_ready, so_done = (sem(s) for s in ("qm_ready", "km_ready", "ss_done", "sn_ready", "so_done"))
    sig_done, val_ready, hi_val = sem("sig_done"), sem("val_ready"), sem("hi_val")

    block = ctx.enter_context(nc.Block())

    def diag(t, row):
        a = t[:, 0, 0:4]
        return bass.AP(a.tensor, a.offset + 0, [list(a.ap[0]), [256, 4], [36, 8], [1, 4]])

    @block.sync
    def _(sp):
        sp.dma_start(FIX[:], consts_fixed).then_inc(consts_in, 16)
        sp.dma_start(XIN[:, 0:TT - 1, :], x_prompt[0].rearrange("(t p) d -> p t d", p=P)).then_inc(x_in, 16)
        sp.dma_start(XIN[0:NS, TT - 1, :], x_sample.rearrange("b l d -> (b l) d")).then_inc(x_in, 16)
        sp.dma_start(GIN[0:16, :], g_mix.rearrange("l (m p) -> (l m) p", p=P)).then_inc(g_in, 16)
        sp.dma_start(GIN[16:32, :], g_ffn.rearrange("l (m p) -> (l m) p", p=P)).then_inc(g_in, 16)
        sp.dma_start(GIN[32:40, :], g_final.rearrange("(m p) -> m p", p=P)).then_inc(g_in, 16)
        with sp.Fori(0, DEPTH) as lay:
            def unit(u, slot, parts):
                sp.wait_ge(lo_ready, lay * NU + u + 1)
                for dst, src in parts:
                    sp.dma_start(dst, src).then_inc(landed[slot], 16)

            def rows(w, k0, k):
                return w[bass.ds(lay, 1), k0 * P:(k0 + k) * P, :].rearrange("o (k p) c -> p (o k) c", p=P)

            def full(u, slot, w, k, col):
                dst = RAW[:, slot, 0:k * UC].rearrange("p (k c) -> p k c", c=UC)
                h = k // 2
                unit(u, slot, [(dst[:, 0:h], rows(w, 0, h)[:, :, bass.ds(col, UC)]),
                               (dst[:, h:k], rows(w, h, h)[:, :, bass.ds(col, UC)])])

            def run(name, w, col, count, skip=0):
                with sp.Fori(0, count) as i:
                    for j in range(2):
                        full(U0[name] + skip + 2 * i + j, j, w, KT, col + (2 * i + j) * UC)

            run("mqk", w_in, C_MQ, 2)
            run("mv", w_in, C_MV, 1)
            run("rqk", w_in, C_RQ, 2)
            run("rv", w_in, C_RV, 2)
            run("rg", w_in, C_RG, 2)
            with sp.Fori(0, 4) as i:
                full(U0["br_ret"] + 2 * i, 0, w_in, KT, C_GR + i * UC)
                full(U0["br_ret"] + 2 * i + 1, 1, w_br_ret, KT, i * UC)
            with sp.Fori(0, 4) as i:
                full(U0["br_att"] + 2 * i, 0, w_in, KT, C_GA + i * UC)
                full(U0["br_att"] + 2 * i + 1, 1, w_br_att, 4, i * UC)
            run("out", w_out, 0, 2)
            with sp.Fori(0, FT // 2) as i:
                for j in range(2):
                    dst = RAW[:, j, :].rearrange("p (k c) -> p k c", c=UC)
                    src = rows(w_gu, 0, KT)
                    col = (2 * i + j) * P
                    unit(U0["gu"] + 2 * i + j, j, [(dst[:, :, 0:P], src[:, :, bass.ds(col, P)]),
                                                   (dst[:, :, P:UC], src[:, :, bass.ds(col + D_FF, P)])])
            with sp.Fori(0, KT) as m:
                for j in range(2):
                    dst = RAW[:, j, 0:11 * P].rearrange("p (k c) -> p k c", c=P)
                    src = rows(w_down, 11 * j, 11)[:, :, bass.ds(m * P, P)]
                    unit(U0["down"] + 2 * m + j, j, [(dst[:, 0:6], src[:, 0:6]), (dst[:, 6:11], src[:, 6:11])])
        for t in range(TT):
            sp.wait_ge(o_scaled, DEPTH * 5 + t + 1)
            n = ROWS[t]
            dst = y_prompt[0, t * P:(t + 1) * P, :] if t < TT - 1 else y_sample.rearrange("b l d -> (b l) d")
            sp.dma_start(dst, YO[0:n, t % 2, :]).then_inc(y_out, 16)
            if t < TT - 2:
                sp.wait_ge(y_out, 16 * (t + 1))
        sp.wait_ge(y_out, 16 * TT)

    @block.gpsimd
    def _(pool):
        pool.dma_start(PTAB[:], page_table.rearrange("b n -> (b n)").unsqueeze(0)).then_inc(ptab_in, 16)
        pool.memset(MHALF, -0.5).then_inc(mhalf_set, 1)
        pool.wait_ge(mhalf_set, 1)
        pool.memset(SM[:, 89:90], 0.0).then_inc(tile_done, 1)
        pool.memset(SM[:, 87:88], 0.0).then_inc(tile_free, 3)
        pool.memset(SM[:, 88:89], 0.0).then_inc(rot_free, 2)
        hold(pool, ptab_in, 16)

        def norm(count):
            hold(pool, nvar, count)
            pool.tensor_tensor(RT, VAR, MHALF, ALU.pow).then_inc(nrt, 1)

        norm(1)
        with pool.Fori(0, DEPTH) as lay:
            hold(pool, tile_done, lay * NT + 1)
            pool.dma_start(CL[:], consts_layer).then_inc(cl_in, 16)

            def page_quad(r):
                g, kv, p = r // 16, r % 16 // 8, r % 8
                if r >= 2:
                    q = r - 2
                    qg, qkv, qp = q // 16, q % 16 // 8, q % 8
                    if qkv == 0:
                        hold(pool, kt_done, lay * 64 + 4 * (qg * 8 + qp + 1))
                    else:
                        hold(pool, pvs_page, lay * 16 + qg * 8 + qp + 1)
                for b in range(GRP):
                    e = (g * GRP + b) * N_PAGES + p
                    page = pool.value_load(PTAB[0:1, e:e + 1], min_val=0, max_val=cache_k.shape[1] - 1)
                    src = (cache_k, cache_v)[kv][bass.ds(lay, 1), bass.ds(page, 1)]
                    pool.dma_start(PG[:, r % 2, b, :], src.rearrange("o n p h d -> p (o n h d)"))\
                        .then_inc(page_in[r % 2], 16)

            page_quad(0)
            page_quad(1)
            hold(pool, rot_free, lay * 40 + 22)
            pool.dma_start(k_prompt[bass.ds(lay, 1)].rearrange("o b (t p) h d -> p (o b t) (h d)", p=P),
                           QK[:, 0:TT - 1, 512:1024]).then_inc(kv_out, 16)
            pool.dma_start(k_sample[bass.ds(lay, 1)].rearrange("o b l h d -> (o b l) (h d)"),
                           QK[0:NS, TT - 1, 512:1024]).then_inc(kv_out, 16)
            hold(pool, tile_free, lay * NT + T0["rqk"] + 2)
            pool.dma_start(v_prompt[bass.ds(lay, 1)].rearrange("o b (t p) h d -> p (o b t) (h d)", p=P),
                           MV[:, 0:TT - 1, :]).then_inc(kv_out, 16)
            pool.dma_start(v_sample[bass.ds(lay, 1)].rearrange("o b l h d -> (o b l) (h d)"),
                           MV[0:NS, TT - 1, :]).then_inc(kv_out, 16)
            for r in range(2, 32):
                page_quad(r)
            for c in range(TT):
                if c == TT - 1:
                    hold(pool, st_ready, lay * 4 + 4)
                    pool.dma_start(state_prompt[bass.ds(lay, 1)].rearrange("o b h k v -> k (o b h) v"), ST[:])\
                        .then_inc(st_out, 16)
                    hold(pool, ot_done, lay * 5 + 4)
                    for b in range(2):
                        pool.dma_start(S0[:, b], state_ret[bass.ds(lay, 1), b].rearrange("o h k v -> k (o h) v"))\
                            .then_inc(s0_in[b], 16)
                    for b in range(DEC_B):
                        hold(pool, sn_ready, lay * 8 + b + 1)
                        pool.dma_start(state_sample[bass.ds(lay, 1), b].rearrange("o h k v -> k (o h) v"),
                                       SN[:, b % 2]).then_inc(sn_out[b % 2], 16)
                        if b + 2 < DEC_B:
                            pool.dma_start(S0[:, b % 2],
                                           state_ret[bass.ds(lay, 1), b + 2].rearrange("o h k v -> k (o h) v"))\
                                .then_inc(s0_in[b % 2], 16)
                hold(pool, var_ready, lay * 5 + c + 1)
                w = 4 if c < TT - 1 else 1
                pool.tensor_tensor(RRS[:, 0:w], RMS[:, 0:w], MHALF[:, 0:w], ALU.pow).then_inc(rms_ready, 1)
            norm(2 * lay + 2)
            norm(2 * lay + 3)
        hold(pool, kv_out, DEPTH * 64)
        hold(pool, st_out, DEPTH * 16)
        hold(pool, sn_out[0], DEPTH * 64)
        hold(pool, sn_out[1], DEPTH * 64)

    @block.tensor
    def _(pe):
        def norm(count):
            pe.wait_ge(sq_added, 8 * count)
            for t, n in enumerate(ROWS):
                last = pe.matmul(PS[0:n, 4, t:t + 1], EB[:, 1, t * P:t * P + n], ONES[:, 0:1], start=True, stop=True)
            last.then_inc(nsum, 1)
            pe.wait_ge(ndiag, count)
            for t in range(TT - 1):
                pe.matmul(PS[:, 5, t * P:(t + 1) * P], ONES, DIAG[:, t, :], start=True, stop=True)
            pe.matmul(PS[:, 6, 0:NS], ONES[0:NS, :], DIAG[0:NS, TT - 1, 0:NS], start=True, stop=True).then_inc(nbc, 1)

        pe.wait_ge(consts_in, 16)
        pe.wait_ge(g_in, 48)
        pe.transpose(PS[:, 0, 0:40], GIN[:], IDENT[0:40, 0:40]).then_inc(xt_done, 1)
        pe.wait_ge(x_in, 32)
        for m in range(KT):
            if m >= 2:
                pe.wait_ge(xt_copied, m)
            for t, n in enumerate(ROWS):
                bank = 4 + 2 * (m % 2) + (t == TT - 1)
                dst = PS[:, bank, t * P:(t + 1) * P] if t < TT - 1 else PS[:, bank, 0:NS]
                last = pe.transpose(dst, XIN[0:n, t, m * P:(m + 1) * P], IDENT[0:n, 0:n])
            last.then_inc(xt_done, 1)
        norm(1)

        with pe.Fori(0, DEPTH) as lay:
            def split_ready(u):
                pe.wait_ge(lo_ready, lay * NU + u + 1 + 2)

            def token_tiles(u, slot, n0):
                split_ready(u)
                wh = WH[:, slot, :].rearrange("p (k c) -> p k c", c=UC)
                wl = WL[:, slot, :].rearrange("p (k c) -> p k c", c=UC)
                for t, n in enumerate(ROWS):
                    tile = n0 + t
                    bank = 2 * ((slot * TT + t) % 2)
                    pe.wait_ge(tile_free, lay * NT + tile + 1)
                    for k in range(KT):
                        a, b = XH[:, k, t * P:t * P + n], XL[:, k, t * P:t * P + n]
                        pe.matmul(PS[0:n, bank, 0:UC], a, wh[:, k], start=k == 0, stop=False)
                        pe.matmul(PS[0:n, bank, 0:UC], a, wl[:, k], start=False, stop=False)
                        last = pe.matmul(PS[0:n, bank, 0:UC], b, wh[:, k], start=False, stop=k == KT - 1)
                    last.then_inc(tile_done, 1)

            def feature_tile(tile, pair, slot, cols, c0, kts, rhs, first=True, final=True):
                wh = WH[:, slot, 0:len(kts) * cols].rearrange("p (k c) -> p k c", c=cols)
                wl = WL[:, slot, 0:len(kts) * cols].rearrange("p (k c) -> p k c", c=cols)
                hi, lo = rhs
                if first:
                    pe.wait_ge(tile_free, lay * NT + tile + 1)
                for i, k in enumerate(kts):
                    for a, w, x in ((0, wh, hi), (1, wh, lo), (2, wl, hi)):
                        for h in range(2):
                            last = pe.matmul(PS[:, 2 * pair + h, 0:HALF], w[:, i, c0:c0 + P],
                                             x[:, k, h * HALF:(h + 1) * HALF],
                                             start=first and i == 0 and a == 0,
                                             stop=final and i == len(kts) - 1 and a == 2)
                if final:
                    last.then_inc(tile_done, 1)
                return last

            def unit2(u, slot, tile, kts, rhs):
                split_ready(u)
                feature_tile(tile, 0, slot, UC, 0, kts, rhs)
                feature_tile(tile + 1, 1, slot, UC, P, kts, rhs)

            def transposes(srcs, base):
                for j, src in enumerate(srcs):
                    if j >= 2:
                        done = tr_act if j % 2 == 0 else tr_dve
                        pe.wait_ge(done, lay * 8 + base // 2 + j // 2)
                    for t, n in enumerate(ROWS):
                        bank = 4 + 2 * (j % 2) + (t == TT - 1)
                        dst = PS[:, bank, t * P:(t + 1) * P] if t < TT - 1 else PS[:, bank, 0:NS]
                        last = pe.transpose(dst, src[0:n, t], IDENT[0:n, 0:n])
                    last.then_inc(tr_done, 1)
                pe.wait_ge(tr_act, lay * 8 + base // 2 + 4)
                pe.wait_ge(tr_dve, lay * 8 + base // 2 + 4)

            with pe.Fori(0, 3) as i:
                for j in range(2):
                    token_tiles(2 * i + j, j, T0["mqk"] + (2 * i + j) * TT)
            pe.wait_ge(rot_free, lay * 40 + 22)
            transposes([QK[:, :, j * P:(j + 1) * P] for j in range(8)], 0)
            pe.wait_ge(tile_free, lay * NT + T0["rqk"] + 2)

            def scores(n):
                h, t = divmod(n, 4)
                r = slice(64 * (h % 2), 64 * (h % 2) + 64)
                if n >= 2:
                    pe.wait_ge(s_exp, lay * 32 + n - 1)
                pe.matmul(PS[:, 4 + n % 2, 0:(t + 1) * P], MT[r, h // 2, t * P:(t + 1) * P],
                          MT[r, 4 + h // 2, 0:(t + 1) * P], start=True, stop=True).then_inc(s_done, 1)

            scores(0)
            for n in range(32):
                h, t = divmod(n, 4)
                if n + 1 < 32:
                    scores(n + 1)
                pe.wait_ge(s_prob, lay * 32 + n + 1)
                if n >= 2:
                    pe.wait_ge(pt_evac, lay * 32 + n - 1)
                for kt in range(t + 1):
                    last = pe.transpose(PS[:, 6 * (1 - n % 2), kt * P:(kt + 1) * P],
                                        PR[:, n % 2, kt * P:(kt + 1) * P], IDENT)
                last.then_inc(pt_done, 1)
                if t == 3:
                    hp = h // 2
                    pe.wait_ge(pt_evac, lay * 32 + n + 1)
                    if h % 2 == 0 and hp >= 2:
                        pe.wait_ge(mo_lo, lay * 4 + hp - 1)
                    for kt in range(4):
                        last = pe.matmul(PS[64 * (h % 2):64 * (h % 2) + 64, 1 + 6 * (hp % 2), kt * P:SEQ],
                                         MV[:, kt, h * 64:(h + 1) * 64], PT[:, h % 2, kt, kt * P:SEQ],
                                         start=kt == 0, stop=kt == 3)
                    if h % 2:
                        last.then_inc(pv_done, 1)

            pe.wait_ge(mo_lo, lay * 4 + 4)
            pe.wait_ge(qb_ready, lay + 1)
            for g in range(NG):
                if g:
                    pe.wait_ge(mos_lo, lay * 2 + g)
                for p in range(N_PAGES):
                    r, q = g * 16 + p, g * 8 + p
                    pe.wait_ge(page_in[r % 2], (lay * 16 + r // 2 + 1) * 64)
                    for b in range(GRP):
                        if q:
                            done = kt_act if b % 2 == 0 else kt_dve
                            pe.wait_ge(done, lay * 32 + 2 * (q - 1) + b // 2 + 1)
                        for hp in range(4):
                            last = pe.transpose(PS[:, b, hp * P:(hp + 1) * P],
                                                PG[:, r % 2, b, hp * P:(hp + 1) * P], IDENT)
                        last.then_inc(kt_done, 1)
                    pe.wait_ge(kt_act, lay * 32 + 2 * q + 2)
                    pe.wait_ge(kt_dve, lay * 32 + 2 * q + 2)
                    for hp in range(4):
                        for b in range(GRP):
                            last = pe.matmul(PS[32 * b:32 * b + 32, 4 + p // 4, (p % 4) * P:(p % 4 + 1) * P],
                                             QB[:, hp, (g * GRP + b) * 32:(g * GRP + b + 1) * 32],
                                             KTT[:, b, hp, :], start=hp == 0, stop=hp == 3)
                    last.then_inc(sc_done, 1)
                for hp in range(4):
                    for b in range(GRP):
                        last = pe.matmul(PS[32 * b:32 * b + 32, 6, 0:NS],
                                         QB[:, hp, (g * GRP + b) * 32:(g * GRP + b + 1) * 32],
                                         MT[:, 4 + hp, SEQ:N], start=hp == 0, stop=hp == 3)
                last.then_inc(sc_done, 1)
                pe.wait_ge(e_done, lay * 2 + g + 1)
                for p in range(N_PAGES):
                    pe.transpose(PS[:, p // 4, (p % 4) * P:(p % 4 + 1) * P], SP_[:, p * P:(p + 1) * P], IDENT)
                pe.transpose(PS[0:NS, 2, 0:P], SP_[:, PAST:PAST + NS], IDENT).then_inc(pts_done, 1)
                pe.wait_ge(pts_act, lay * 2 + g + 1)
                pe.wait_ge(pts_dve, lay * 2 + g + 1)
                for p in range(N_PAGES):
                    r = g * 16 + 8 + p
                    pe.wait_ge(page_in[r % 2], (lay * 16 + r // 2 + 1) * 64)
                    for b in range(GRP):
                        last = pe.matmul(PS[32 * b:32 * b + 32, 7, :], PTS[:, p, 32 * b:32 * b + 32],
                                         PG[:, r % 2, b, :], start=p == 0, stop=False)
                    last.then_inc(pvs_page, 1)
                for b in range(GRP):
                    last = pe.matmul(PS[32 * b:32 * b + 32, 7, :], PTS[0:NS, 8, 32 * b:32 * b + 32],
                                     MV[0:NS, TT - 1, :], start=False, stop=True)
                last.then_inc(pts_done, 1)
                pe.wait_ge(os_ready, lay * 2 + g + 1)
                for hp in range(4):
                    last = pe.matmul(PS[:, 3, hp * 16:(hp + 1) * 16], OS[:, hp * P:(hp + 1) * P],
                                     cl("sel"), start=True, stop=True)
                last.then_inc(mos_done, 1)
            hold(pe, mos_lo, lay * 2 + 2)

            with pe.Fori(0, 4) as i:
                for j in range(2):
                    token_tiles(U0["rqk"] + 2 * i + j, j, T0["rqk"] + (2 * i + j) * TT)
            pe.wait_ge(rot_free, lay * 40 + 42)
            transposes([RQ[:, :, j * P:(j + 1) * P] for j in range(4)]
                       + [RK[:, :, j * P:(j + 1) * P] for j in range(4)], 8)
            pe.wait_ge(tile_free, lay * NT + T0["rg"] + 2)

            def inner(c):
                if c:
                    pe.wait_ge(in_masked, lay * 5 + c)
                for h in range(R_HEADS):
                    last = pe.matmul(PS[:, 4, h * P:(h + 1) * P], RTT[:, 4 + h, c * P:(c + 1) * P],
                                     RTT[:, h, c * P:(c + 1) * P], start=True, stop=True)
                last.then_inc(in_done, 1)

            def chunk(c):
                pe.wait_ge(in_masked, lay * 5 + c + 1)
                if c:
                    pe.wait_ge(o_scaled, lay * 5 + c)
                    pe.wait_ge(st_ready, lay * 4 + c)
                for h in range(R_HEADS):
                    dst = PS[:, 5 + h // 2, (h % 2) * 256:(h % 2 + 1) * 256]
                    last = pe.matmul(dst, IND[:, h * P:(h + 1) * P], RV[:, c, h * 256:(h + 1) * 256],
                                     start=True, stop=c == 0)
                    if c:
                        last = pe.matmul(dst, QD[:, h * P:(h + 1) * P], ST[:, h, :], start=False, stop=True)
                last.then_inc(o_done, 1)
                pe.wait_ge(kd_ready, lay * 5 + c + 1)
                for h in range(R_HEADS):
                    last = pe.matmul(PS[:, 2 + h // 2, (h % 2) * 256:(h % 2 + 1) * 256],
                                     RK[:, c, h * P:(h + 1) * P], RV[:, c, h * 256:(h + 1) * 256],
                                     start=True, stop=True)
                last.then_inc(st_done, 1)

            def turn(c):
                pe.wait_ge(o_scaled, lay * 5 + c + 1)
                if c:
                    pe.wait_ge(ot_act, lay * 5 + c)
                    pe.wait_ge(ot_dve, lay * 5 + c)
                for j in range(8):
                    last = pe.transpose(PS[:, j // 4, (j % 4) * P:(j % 4 + 1) * P], RV[:, c, j * P:(j + 1) * P], IDENT)
                last.then_inc(ot_done, 1)

            inner(0)
            for c in range(4):
                chunk(c)
                if c < 3:
                    inner(c + 1)
                if c:
                    turn(c - 1)
            turn(3)
            pe.wait_ge(in_masked, lay * 5 + 4)
            pe.wait_ge(o_scaled, lay * 5 + 4)
            for h in range(R_HEADS):
                last = pe.matmul(PS[0:NS, 4, h * NS:(h + 1) * NS], RTT[:, 4 + h, SEQ:N], RTT[:, h, SEQ:N],
                                 start=True, stop=True)
            last.then_inc(in_done, 1)
            hold(pe, in_masked, lay * 5 + 5)
            for h in range(R_HEADS):
                pe.matmul(PS[32 * h:32 * h + 32, 5, 0:256], IND[0:NS, h * NS:(h + 1) * NS],
                          RV[0:NS, TT - 1, h * 256:(h + 1) * 256], start=True, stop=False)
            pe.wait_ge(qm_ready, lay + 1)
            for b in range(DEC_B):
                pe.wait_ge(s0_in[b % 2], (lay * 4 + b // 2 + 1) * 16)
                for h in range(R_HEADS):
                    last = pe.matmul(PS[32 * h:32 * h + 32, 5, 0:256], QM[:, h, b * 32:(b + 1) * 32],
                                     S0[:, b % 2, h, :], start=False, stop=b == DEC_B - 1)
                if b == DEC_B - 1:
                    last.then_inc(so_done, 1)
                pe.wait_ge(km_ready, lay * 8 + b + 1)
                if b:
                    pe.wait_ge(sn_ready, lay * 8 + b)
                for h in range(R_HEADS):
                    last = pe.matmul(PS[:, 2 + h // 2, (h % 2) * 256:(h % 2 + 1) * 256],
                                     KM[0:NS, b % 2, h * P:(h + 1) * P], RV[0:NS, TT - 1, h * 256:(h + 1) * 256],
                                     start=True, stop=True)
                last.then_inc(ss_done, 1)
            pe.wait_ge(o_scaled, lay * 5 + 5)
            pe.wait_ge(ot_act, lay * 5 + 4)
            pe.wait_ge(ot_dve, lay * 5 + 4)
            for j in range(2):
                last = pe.transpose(PS[:, j, 0:P], EA[:, 0, j * P:(j + 1) * P], IDENT)
            last.then_inc(ot_done, 1)
            hold(pe, ot_act, lay * 5 + 5)
            hold(pe, ot_dve, lay * 5 + 5)

            x = (XH, XL)
            kk = list(range(KT))
            with pe.Fori(0, 2) as i:
                for j in range(2):
                    unit2(U0["rg"] + 2 * i + j, j, T0["rg"] + 4 * i + 2 * j, kk, x)
            for name, rhs, ks in (("br_ret", (ROH, ROL), kk), ("br_att", (MOH, MOL), kk[:4])):
                hold(pe, x_lo, lay * NX + 16)
                with pe.Fori(0, 4) as i:
                    unit2(U0[name] + 2 * i, 0, T0[name] + 4 * i, kk, x)
                    unit2(U0[name] + 2 * i + 1, 1, T0[name] + 4 * i + 2, ks, rhs)
            hold(pe, x_lo, lay * NX + 24)
            with pe.Fori(0, 2) as i:
                for j in range(2):
                    unit2(U0["out"] + 2 * i + j, j, T0["out"] + 4 * i + 2 * j, kk, (ROH, ROL))
            norm(2 * lay + 2)
            with pe.Fori(0, FT // 2) as i:
                for j in range(2):
                    unit2(U0["gu"] + 2 * i + j, j, T0["gu"] + 4 * i + 2 * j, kk, x)
            hold(pe, x_lo, lay * NX + 54)
            with pe.Fori(0, KT // 2) as i:
                for m in range(2):
                    for j in range(2):
                        u, tile = U0["down"] + 4 * i + 2 * m + j, T0["down"] + 2 * i + m
                        split_ready(u)
                        last = feature_tile(tile, m, j, P, 0, range(11 * j, 11 * j + 11), (AH, AL), j == 0, j == 1)
                        if j == 0:
                            last.then_inc(half_done, 1)
            norm(2 * lay + 3)

        for t, n in enumerate(ROWS):
            pe.wait_ge(xg_ready, 1)
            if t >= 2:
                pe.wait_ge(o_scaled, DEPTH * 5 + t - 1)
            for m in range(KT):
                last = pe.transpose(PS[0:n, 4 + 2 * (t % 2) + m // 4, (m % 4) * P:(m % 4 + 1) * P],
                                    XT[:, m, t * P:t * P + n], IDENT)
            last.then_inc(tr_done, 1)

    @block.scalar
    def _(act):
        def x_parts(m, gcol, ready, squared):
            hold(act, *ready)
            act.activation(XH[:, m, :], XT[:, m, :], ACT.Copy, scale=GT[:, gcol])
            hold(act, sq_added, squared)
            act.activation(EB[:, 0, :], XT[:, m, :], ACT.Square).then_inc(hi_val, 1)

        act.wait_ge(g_ready, 1)
        for m in range(KT):
            x_parts(m, slice(m, m + 1), (xt_copied, m + 1), m)

        with act.Fori(0, DEPTH) as lay:
            def split(u, slot, n, prev):
                act.wait_ge(landed[slot], (lay * NU // 2 + u // 2 + 1) * 32 if isinstance(u, int)
                            else lay * (NU * 16) + u * 16 + (32 - 16 * slot))
                act.wait_ge(*prev)
                act.activation(WH[:, slot, 0:n], RAW[:, slot, 0:n], ACT.Copy).then_inc(hi_ready, 1)

            def ahead(name, i, j, per, n=8 * UC):
                split(2 * i + (U0[name] + j + 1), (j + 1) % 2, n,
                      (tile_done, lay * NT + T0[name] + per * j + i * (2 * per)))

            def done(tile):
                act.wait_ge(tile_done, lay * NT + tile + 1)

            def rotated_tiles(name, i, j, scale, r0):
                for t, n in enumerate(ROWS):
                    tile = i * (2 * TT) + (T0[name] + j * TT + t)
                    bank = (j * TT + t) % 2
                    done(tile)
                    act.wait_ge(rot_free, lay * 40 + i * (2 * TT) + (r0 + j * TT + t + 1))
                    act.activation(XS[0:n, bank, :], PS[0:n, 2 * bank, 0:UC], ACT.Copy,
                                   scale=scale[0:n, t:t + 1]).then_inc(tile_free, 1)

            def value_tiles(name, i, j, dst):
                for t, n in enumerate(ROWS):
                    hold(act, tile_done, lay * NT + i * (2 * TT) + (T0[name] + j * TT + t + 1))
                    act.activation(dst[0:n, t, bass.ds(i * (2 * UC) + j * UC, UC)], PS[0:n, 2 * ((j * TT + t) % 2), 0:UC],
                                   ACT.Copy, scale=RT[0:n, t:t + 1]).then_inc(tile_free, 1)

            def copy_transposes(dst, base):
                for j in range(0, 8, 2):
                    act.wait_ge(tr_done, lay * 16 + base + j + 1)
                    act.activation(dst[:, j, 0:SEQ], PS[:, 4, :], ACT.Copy)
                    act.activation(dst[:, j, SEQ:N], PS[:, 5, 0:NS], ACT.Copy).then_inc(tr_act, 1)

            split(0, 0, 8 * UC, (tile_done, lay * NT + 1))
            act.wait_ge(ndiag, 2 * lay + 1)
            with act.Fori(0, 2) as i:
                for j in range(2):
                    ahead("mqk", i, j, TT)
                    rotated_tiles("mqk", i, j, RT, 0)
            for j in range(2):
                ahead("mv", 0, j, TT)
                value_tiles("mv", 0, j, MV)
            copy_transposes(MT, 0)

            def exp(n):
                w = (n % 4 + 1) * P
                act.wait_ge(s_max, lay * 32 + n + 1)
                if n >= 2:
                    act.wait_ge(pt_done, lay * 32 + n - 1)
                act.activation(PR[:, n % 2, 0:w], PS[:, 4 + n % 2, 0:w], ACT.Exp, bias=NM[:, n % 2:n % 2 + 1],
                               scale=M_SCALE, accum_out=RSUM[:, n % 2:n % 2 + 1]).then_inc(s_exp, 1)

            act.wait_ge(kv_out, lay * 64 + 64)
            exp(0)
            for n in range(32):
                h, t = divmod(n, 4)
                if n + 1 < 32:
                    exp(n + 1)
                act.wait_ge(pt_done, lay * 32 + n + 1)
                act.activation(PT[:, h % 2, 0:t + 1, t * P:(t + 1) * P],
                               PS[:, 6 * (1 - n % 2), 0:(t + 1) * P].rearrange("p (k c) -> p k c", c=P),
                               ACT.Copy).then_inc(pt_evac, 1)
                if t == 3 and h % 2:
                    hp = h // 2
                    act.wait_ge(pv_done, lay * 4 + hp + 1)
                    act.activation(MOH[:, hp, 0:SEQ], PS[:, 1 + 6 * (hp % 2), :], ACT.Copy).then_inc(mo_hi, 1)

            for g in range(NG):
                for p in range(N_PAGES):
                    q = g * 8 + p
                    for b in (0, 2):
                        act.wait_ge(kt_done, lay * 64 + 4 * q + b + 1)
                        if q:
                            act.wait_ge(sc_done, lay * 18 + 9 * g + p)
                        act.activation(KTT[:, b, :, :], PS[:, b, :].rearrange("p (k c) -> p k c", c=P),
                                       ACT.Copy).then_inc(kt_act, 1)
                act.wait_ge(sel_ready, lay * 2 + g + 1)
                for k in range(4):
                    act.activation(SP_[:, k * 256:(k + 1) * 256], PS[:, 4 + k // 2, (k % 2) * 256:(k % 2 + 1) * 256],
                                   ACT.Exp, bias=BIAS[:, k:k + 1], scale=M_SCALE, accum_out=ES[:, k:k + 1])
                act.activation(SP_[:, PAST:PAST + NS], PS[:, 6, 0:NS], ACT.Exp, bias=BIAS[:, 4:5], scale=M_SCALE,
                               accum_out=ES[:, 4:5]).then_inc(e_done, 1)
                act.wait_ge(pts_done, lay * 4 + 2 * g + 1)
                act.activation(PTS[:, 0:4, :], PS[:, 0, :].rearrange("p (k c) -> p k c", c=P), ACT.Copy)\
                    .then_inc(pts_act, 1)
                act.wait_ge(mos_done, lay * 2 + g + 1)
                act.activation(MOH[:, :, SEQ + 16 * g:SEQ + 16 * (g + 1)],
                               PS[:, 3, 0:64].rearrange("p (k c) -> p k c", c=16), ACT.Copy).then_inc(mos_hi, 1)

            for j in range(2):
                ahead("rqk", 0, j, TT)
                rotated_tiles("rqk", 0, j, RT, 20)
            for j in range(2):
                ahead("rqk", 1, j, TT)
                rotated_tiles("rqk", 1, j, RTK, 20)
            with act.Fori(0, 2) as i:
                for j in range(2):
                    ahead("rv", i, j, TT)
                    value_tiles("rv", i, j, RV)
            copy_transposes(RTT, 8)

            def scale_out(c, src, dst, k):
                act.wait_ge(o_done if c < 4 else so_done, lay * 4 + c + 1 if c < 4 else lay + 1)
                for h in range(k):
                    last = act.activation(EB[:].rearrange("p a n -> p (a n)")[:, h * 256:(h + 1) * 256], src(h), ACT.Square, accum_out=SSQ[:, h:h + 1])
                last.then_inc(ssq_ready, 1)
                act.wait_ge(rms_ready, lay * 5 + c + 1)
                if c < 4:
                    act.wait_ge(st_done, lay * 4 + c + 1)
                for h in range(k):
                    last = act.activation(dst(h), src(h), ACT.Copy, scale=RRS[:, h:h + 1])
                last.then_inc(o_scaled, 1)

            def out_turned(c):
                act.wait_ge(ot_done, lay * 5 + c + 1)
                act.activation(ROT[:, 0:4, c * P:(c + 1) * P], PS[:, 0, :].rearrange("p (k c) -> p k c", c=P),
                               ACT.Copy).then_inc(ot_act, 1)

            for c in range(4):
                scale_out(c, lambda h: PS[:, 5 + h // 2, (h % 2) * 256:(h % 2 + 1) * 256],
                          lambda h: RV[:, c, h * 256:(h + 1) * 256], R_HEADS)
                if c:
                    out_turned(c - 1)
            out_turned(3)
            scale_out(4, lambda h: PS[:, 5, 0:256], lambda h: EA[:, 0, 0:256], 1)
            act.wait_ge(ot_done, lay * 5 + 5)
            act.activation(ROT[:, 0:8:2, SEQ:N], PS[:, 0, 0:P].rearrange("p (h c) -> p h c", c=NS),
                           ACT.Copy).then_inc(ot_act, 1)

            def sig(tile, dst, src, e):
                act.wait_ge(tile_free, lay * NT + tile + 3)
                act.activation(EB[:, dst, :], EA[:, src, :], ACT.Sigmoid).then_inc(sig_done, 1)

            act.wait_ge(st_out, lay * 16 + 16)
            for b in range(2):
                act.wait_ge(sn_out[b], lay * 64 + 64)
            with act.Fori(0, 2) as i:
                for j in range(2):
                    ahead("rg", i, j, 2)
                    for m in range(2):
                        k = 4 * i + (2 * j + m)
                        sig(k + T0["rg"], m, m, k)
                        hold(act, val_ready, lay * NVAL + k + (V0N["rg"] + 1))
                        act.activation(ROH[:, bass.ds(k, 1), :], EA[:, m:m + 1, :], ACT.Copy).then_inc(hi_val, 1)
            with act.Fori(0, 4) as i:
                for j in range(2):
                    ahead("br_ret", i, j, 2)
                    if j == 0:
                        for m in range(2):
                            sig(4 * i + (T0["br_ret"] + m), m, m, 0)
            with act.Fori(0, 4) as i:
                for j in range(2):
                    ahead("br_att", i, j, 2, 4 * UC if j == 0 else 8 * UC)
                    for m in range(2):
                        if j == 0:
                            sig(4 * i + (T0["br_att"] + m), m, m, 0)
                        else:
                            hold(act, val_ready, lay * NVAL + 2 * i + (V0N["br_att"] + m + 1))
                            act.activation(ROH[:, bass.ds(2 * i + m, 1), :], G1[:, bass.ds(2 * i + m, 1), :],
                                           ACT.Copy).then_inc(hi_val, 1)
            with act.Fori(0, 2) as i:
                for j in range(2):
                    ahead("out", i, j, 2)
                    for m in range(2):
                        k = 4 * i + (2 * j + m)
                        x_parts(bass.ds(k, 1), bass.ds(8 * lay + k + 16, 1),
                                (tile_free, lay * NT + k + (T0["out"] + 3)), (2 * lay + 1) * KT + k)
            with act.Fori(0, FT // 2) as i:
                for j in range(2):
                    ahead("gu", i, j, 2)
                    sig(4 * i + (2 * j + T0["gu"]), 0, 0, 0)
                    hold(act, val_ready, lay * NVAL + 2 * i + (V0N["gu"] + j + 1))
                    act.activation(AH[:, bass.ds(2 * i + j, 1), :], EA[:, 1:2, :], ACT.Copy).then_inc(hi_val, 1)

            def down(i, m, last=False):
                k = 2 * i + m
                split(4 * i + (U0["down"] + 2 * m + 1), 1, 11 * P, (tile_done, lay * NT + k + T0["down"]))
                if not last:
                    split(4 * i + (U0["down"] + 2 * m + 2), 0, 8 * UC, (half_done, lay * KT + k + 1))
                x_parts(bass.ds(k, 1), bass.ds(24 * lay + k + 8, 1),
                        (tile_free, lay * NT + k + (T0["down"] + 3)), (2 * lay + 2) * KT + k)

            with act.Fori(0, KT // 2 - 1) as i:
                for m in range(2):
                    down(i, m)
            down(KT // 2 - 1, 0)
            down(KT // 2 - 1, 1, True)

        for t, n in enumerate(ROWS):
            act.wait_ge(tr_done, DEPTH * 16 + t + 1)
            if t == 0:
                act.wait_ge(nrt, 2 * DEPTH + 1)
            if t >= 2:
                act.wait_ge(y_out, 16 * (t - 1))
            act.activation(YO[0:n, t % 2, :].rearrange("p (a c) -> p a c", a=2),
                           PS[0:n, 4 + 2 * (t % 2):6 + 2 * (t % 2), :], ACT.Copy,
                           scale=RT[0:n, t:t + 1]).then_inc(o_scaled, 1)

    @block.vector
    def _(dve):
        own = Order(dve, dve_own)
        pair = [PS[:, 2 * p:2 * p + 2, 0:HALF] for p in range(2)]

        def halves(a):
            return a.rearrange("p (h c) -> p h c", h=2)

        RB = halves(RSTDB[:])

        def norm(count):
            dve.wait_ge(nsum, count)
            dve.tensor_scalar(VAR[:, 0:TT - 1], PS[:, 4, 0:TT - 1], 1.0 / D_MODEL, EPS, ALU.mult, ALU.add)
            dve.tensor_scalar(VAR[0:NS, TT - 1:TT], PS[0:NS, 4, TT - 1:TT], 1.0 / D_MODEL, EPS,
                              ALU.mult, ALU.add).then_inc(nvar, 1)
            dve.wait_ge(nrt, count)
            dve.tensor_scalar(RTK, RT, R_DK ** -0.5, None, ALU.mult)
            dve.tensor_tensor(DIAG, IDENT.unsqueeze(1).to_broadcast([P, TT, P]),
                              RT.unsqueeze(2).to_broadcast([P, TT, P]), ALU.mult).then_inc(ndiag, 1)
            dve.wait_ge(nbc, count)
            dve.tensor_copy(RSTDB[:, 0:SEQ], PS[:, 5, :])
            own.mark(dve.tensor_copy(RSTDB[:, SEQ:N], PS[:, 6, 0:NS]))

        def low_x(m, gcol, hi, squared):
            dve.wait_ge(hi_val, hi)
            dve.scalar_tensor_tensor(out=XL[:, m, :], in0=XT[:, m, :], scalar=GT[:, gcol],
                                     in1=XH[:, m, :].bitcast(F32), op0=ALU.mult, op1=ALU.subtract).then_inc(x_lo, 1)
            dve.wait_ge(sq_added, squared)
            dve.tensor_tensor(EB[:, 1, :], EB[:, 1, :], EB[:, 0, :], ALU.add).then_inc(sq_added, 1)

        own.mark(dve.memset(VAR, 1.0))
        own.mark(dve.memset(EB[:, 1, :], 0.0))
        dve.wait_ge(xt_done, 1)
        dve.tensor_copy(GT[:], PS[:, 0, 0:40]).then_inc(g_ready, 1)
        dve.wait_ge(g_ready, 1)
        own.wait()

        def input_tile(m):
            dve.wait_ge(xt_done, m + 2)
            dve.tensor_copy(XT[:, m, 0:SEQ], PS[:, 4 + 2 * (m % 2), :])
            dve.tensor_copy(XT[:, m, SEQ:N], PS[:, 5 + 2 * (m % 2), 0:NS]).then_inc(xt_copied, 1)

        input_tile(0)
        for m in range(KT):
            if m + 1 < KT:
                input_tile(m + 1)
            low_x(m, slice(m, m + 1), m + 1, m)
        norm(1)
        dve.memset(SM[:, 90:91], 0.0).then_inc(lo_ready, 2)

        with dve.Fori(0, DEPTH) as lay:
            own.base, own.n, start = lay * LAYER_MARKS + own.n, 0, own.n

            def split(u, slot, n):
                dve.wait_ge(hi_ready, lay * NU + u + 1)
                dve.tensor_tensor(WL[:, slot, 0:n], RAW[:, slot, 0:n], WH[:, slot, 0:n].bitcast(F32),
                                  ALU.subtract).then_inc(lo_ready, 1)

            def ahead(name, i, j, n=8 * UC):
                split(2 * i + (U0[name] + j + 1), (j + 1) % 2, n)

            def rotate(src, dst, cos, sin, n, heads, pairs, before):
                s, d = pairs(src), pairs(dst)
                w = s[0].shape[-1]
                c = cos.unsqueeze(1).to_broadcast([n, heads, w])
                z = sin.unsqueeze(1).to_broadcast([n, heads, w])
                a1, a2 = (RO1[0:n, k * 128:(k + 1) * 128].rearrange("p (h w) -> p h w", h=heads) for k in range(2))
                b1, b2 = (RO2[0:n, k * 128:(k + 1) * 128].rearrange("p (h w) -> p h w", h=heads) for k in range(2))
                dve.wait_ge(rot_free, before)
                dve.tensor_tensor(a1, s[0], c, ALU.mult)
                dve.tensor_tensor(a2, s[1], z, ALU.mult)
                dve.tensor_tensor(b1, s[1], c, ALU.mult)
                own.mark(dve.tensor_tensor(b2, s[0], z, ALU.mult))
                own.wait()
                dve.tensor_tensor(d[0], a1, a2, ALU.subtract)
                dve.tensor_tensor(d[1], b1, b2, ALU.add).then_inc(rot_free, 1)

            def rope_pairs(a):
                v = a.rearrange("p (h z w) -> p h z w", z=2, w=32)
                return v[:, :, 0, :], v[:, :, 1, :]

            def retnet_pairs(a):
                v = a.rearrange("p (h w z) -> p h w z", z=2, w=64)
                return v[:, :, :, 0], v[:, :, :, 1]

            def rotated_tiles(name, i, j, dst, col, tables, heads, pairs, r0):
                for t, n in enumerate(ROWS):
                    tile = i * (2 * TT) + (T0[name] + j * TT + t)
                    dve.wait_ge(tile_free, lay * NT + tile + 3)
                    w = tables[0].shape[-1] // TT
                    rotate(XS[0:n, (j * TT + t) % 2, :], dst[0:n, t, bass.ds(col, UC)],
                           tables[0][0:n, t * w:(t + 1) * w], tables[1][0:n, t * w:(t + 1) * w], n, heads, pairs,
                           lay * 40 + i * (2 * TT) + (r0 + j * TT + t + 2))

            def copy_transposes(dst, base):
                for j in range(1, 8, 2):
                    dve.wait_ge(tr_done, lay * 16 + base + j + 1)
                    dve.tensor_copy(dst[:, j, 0:SEQ], PS[:, 6, :])
                    dve.tensor_copy(dst[:, j, SEQ:N], PS[:, 7, 0:NS]).then_inc(tr_dve, 1)

            split(0, 0, 8 * UC)
            hold(dve, cl_in, lay * 16 + 16)
            with own.loop(2, 2 * TT) as i:
                for j in range(2):
                    ahead("mqk", i, j)
                    rotated_tiles("mqk", i, j, QK, i * (2 * UC) + j * UC, (cl("cosm"), cl("sinm")), 4, rope_pairs, 0)
            for j in range(2):
                ahead("mv", 0, j)
            copy_transposes(MT, 0)

            def row_max(n):
                t, b = n % 4, n % 2
                dve.wait_ge(s_done, lay * 32 + n + 1)
                d = PS[:, 4 + b, t * P:(t + 1) * P]
                own.mark(dve.tensor_tensor(d, d, cl("causal"), ALU.add))
                own.wait()
                own.mark(dve.tensor_reduce(MX[:, b:b + 1], PS[:, 4 + b, 0:(t + 1) * P], AX, ALU.max))
                own.wait()
                dve.tensor_scalar(NM[:, b:b + 1], MX[:, b:b + 1], -M_SCALE, None, ALU.mult).then_inc(s_max, 1)

            row_max(0)
            for n in range(32):
                h, t, b = n // 4, n % 4, n % 2
                if n + 1 < 32:
                    row_max(n + 1)
                dve.wait_ge(s_exp, lay * 32 + n + 1)
                own.mark(dve.reciprocal(RINV[:, b:b + 1], RSUM[:, b:b + 1]))
                own.wait()
                p = PR[:, b, 0:(t + 1) * P]
                dve.tensor_scalar(p, p, RINV[:, b:b + 1], None, ALU.mult).then_inc(s_prob, 1)
                if t == 3 and h % 2:
                    hp = h // 2
                    dve.wait_ge(mo_hi, lay * 4 + hp + 1)
                    dve.tensor_tensor(MOL[:, hp, 0:SEQ], PS[:, 1 + 6 * (hp % 2), :], MOH[:, hp, 0:SEQ].bitcast(F32),
                                      ALU.subtract).then_inc(mo_lo, 1)

            dve.wait_ge(kv_out, lay * 64 + 64)
            dve.wait_ge(tr_act, lay * 8 + 4)
            dve.wait_ge(mo_lo, lay * 4 + 4)
            own.mark(dve.memset(QB[:], 0.0))
            own.wait()
            for hp in range(4):
                for z in range(2):
                    r = slice(64 * z, 64 * z + 64)
                    last = dve.tensor_copy(
                        QB[r, hp, :].rearrange("p (b c) -> p b c", c=32)[:, :, 8 * hp + 4 * z:8 * hp + 4 * z + 4],
                        MT[r, hp, SEQ:N].rearrange("p (b q) -> p b q", q=DEC_L))
            last.then_inc(qb_ready, 1)
            for g in range(NG):
                for p in range(N_PAGES):
                    q = g * 8 + p
                    for b in (1, 3):
                        dve.wait_ge(kt_done, lay * 64 + 4 * q + b + 1)
                        if q:
                            dve.wait_ge(sc_done, lay * 18 + 9 * g + p)
                        dve.tensor_copy(KTT[:, b, :, :], PS[:, b, :].rearrange("p (k c) -> p k c", c=P))\
                            .then_inc(kt_dve, 1)
                dve.wait_ge(sc_done, lay * 18 + 9 * g + 9)
                blocks = PS[:, 4:6, :].rearrange("p a (k c) -> p (a k) c", c=M_BLOCK)
                dve.tensor_tensor(PS[:, 6, 0:NS], PS[:, 6, 0:NS], cl("own")[:, g * NS:(g + 1) * NS], ALU.add)
                dve.tensor_reduce(BS, blocks, AX, ALU.add)
                own.mark(dve.tensor_reduce(BM[:, 0:4], blocks, AX, ALU.max))
                own.wait()
                dve.tensor_reduce(BM[:, 4:5], PS[:, 6, 0:NS], AX, ALU.max)
                own.mark(dve.tensor_reduce(T1A[:, 0:1], BS, AX, ALU.min))
                own.wait()
                own.mark(dve.scalar_tensor_tensor(out=EQ, in0=BS, scalar=T1A[:, 0:1], in1=cl("rank"),
                                                  op0=ALU.is_equal, op1=ALU.mult))
                own.wait()
                own.mark(dve.tensor_reduce(T1A[:, 1:2], EQ, AX, ALU.max))
                own.wait()
                own.mark(dve.tensor_scalar(PEN, EQ, T1A[:, 1:2], -BIG, ALU.is_equal, ALU.mult))
                own.wait()
                own.mark(dve.tensor_tensor(BM[:, 0:4], BM[:, 0:4], PEN, ALU.add))
                own.wait()
                own.mark(dve.tensor_reduce(T1A[:, 0:1], BM, AX, ALU.max))
                own.wait()
                own.mark(dve.tensor_scalar(BIAS[:, 4:5], T1A[:, 0:1], -M_SCALE, None, ALU.mult))
                own.wait()
                dve.tensor_scalar(BIAS[:, 0:4], PEN, BIAS[:, 4:5], None, ALU.add).then_inc(sel_ready, 1)
                dve.wait_ge(e_done, lay * 2 + g + 1)
                own.mark(dve.tensor_reduce(SRI, ES, AX, ALU.add))
                own.wait()
                own.mark(dve.reciprocal(SRI, SRI))
                dve.wait_ge(pts_done, lay * 4 + 2 * g + 1)
                dve.tensor_copy(PTS[:, 4:8, :], PS[:, 1, :].rearrange("p (k c) -> p k c", c=P))
                dve.tensor_copy(PTS[0:NS, 8, :], PS[0:NS, 2, 0:P]).then_inc(pts_dve, 1)
                own.wait()
                dve.wait_ge(pts_done, lay * 4 + 2 * g + 2)
                dve.scalar_tensor_tensor(out=OS[:].rearrange("p (h c) -> p h c", c=M_DH),
                                         in0=PS[:, 7, :].rearrange("p (h c) -> p h c", c=M_DH), scalar=SRI,
                                         in1=cl("headm").unsqueeze(2).to_broadcast([P, 8, M_DH]),
                                         op0=ALU.mult, op1=ALU.mult).then_inc(os_ready, 1)
                dve.wait_ge(mos_hi, lay * 2 + g + 1)
                cols = slice(SEQ + 16 * g, SEQ + 16 * (g + 1))
                dve.tensor_tensor(MOL[:, :, cols], PS[:, 3, 0:64].rearrange("p (k c) -> p k c", c=16),
                                  MOH[:, :, cols].bitcast(F32), ALU.subtract).then_inc(mos_lo, 1)

            for k, dst in ((0, RQ), (1, RK)):
                for j in range(2):
                    ahead("rqk", k, j)
                    rotated_tiles("rqk", k, j, dst, j * UC, (cl("cosr"), cl("sinr")), 2, retnet_pairs, 20)
            with own.loop(2, 0) as i:
                for j in range(2):
                    ahead("rv", i, j)
            copy_transposes(RTT, 8)
            dve.wait_ge(tr_done, lay * 16 + 16)
            for t, n in enumerate(ROWS):
                k = RK[0:n, t, :].rearrange("p (h c) -> p h c", c=P)
                dec = (cl("kdec") if t < TT - 1 else cl("kdecs"))[0:n].unsqueeze(2).to_broadcast([n, 4, P])
                dve.tensor_tensor(k, k, dec, ALU.mult).then_inc(kd_ready, 1)
            dve.wait_ge(tr_act, lay * 8 + 8)
            dve.wait_ge(tr_dve, lay * 8 + 8)

            def masked(c):
                dve.wait_ge(in_done, lay * 5 + c + 1)
                if c:
                    dve.wait_ge(o_done, lay * 4 + c)
                    dve.tensor_tensor(QD.rearrange("p (h c) -> p h c", c=P), RTT[:, 0:4, c * P:(c + 1) * P],
                                      cl("qdt").rearrange("p (h c) -> p h c", c=P), ALU.mult)
                dve.tensor_tensor(IND, PS[:, 4, :], cl("dect"), ALU.mult).then_inc(in_masked, 1)

            def variances(c, k):
                dve.wait_ge(ssq_ready, lay * 5 + c + 1)
                dve.tensor_scalar(RMS[:, 0:k], SSQ[:, 0:k], 1.0 / R_DV, EPS, ALU.mult, ALU.add).then_inc(var_ready, 1)

            def out_turned(c):
                dve.wait_ge(ot_done, lay * 5 + c + 1)
                dve.tensor_copy(ROT[:, 4:8, c * P:(c + 1) * P], PS[:, 1, :].rearrange("p (k c) -> p k c", c=P))\
                    .then_inc(ot_dve, 1)

            masked(0)
            for c in range(4):
                variances(c, R_HEADS)
                dve.wait_ge(st_done, lay * 4 + c + 1)
                if c == 0:
                    dve.tensor_copy(ST[:].rearrange("p (a b) c -> p a (b c)", a=2), PS[:, 2:4, :]).then_inc(st_ready, 1)
                else:
                    dve.wait_ge(st_ready, lay * 4 + c)
                    for h in range(R_HEADS):
                        last = dve.scalar_tensor_tensor(
                            out=ST[:, h, :], in0=ST[:, h, :], scalar=G_CHUNK[h],
                            in1=PS[:, 2 + h // 2, (h % 2) * 256:(h % 2 + 1) * 256], op0=ALU.mult, op1=ALU.add)
                    last.then_inc(st_ready, 1)
                if c < 3:
                    masked(c + 1)
                if c:
                    out_turned(c - 1)
            out_turned(3)
            own.mark(dve.memset(QM[:], 0.0))
            own.wait()
            dve.tensor_tensor(diag(QM, 0), RTT[:, 0:4, SEQ:N].rearrange("p h (b q) -> p h b q", q=DEC_L),
                              cl("qds").rearrange("p (h b q) -> p h b q", h=4, q=DEC_L), ALU.mult).then_inc(qm_ready, 1)
            dve.wait_ge(in_done, lay * 5 + 5)
            dve.tensor_tensor(IND[0:NS, 0:P], PS[0:NS, 4, 0:P], cl("decs", NS), ALU.mult).then_inc(in_masked, 1)

            def key_of(b):
                if b >= 2:
                    dve.wait_ge(ss_done, lay * 8 + b - 1)
                dve.tensor_scalar(KM[0:NS, b % 2, :], RK[0:NS, TT - 1, :], cl("seqm", NS)[:, b:b + 1], None,
                                  ALU.mult).then_inc(km_ready, 1)

            dve.wait_ge(kd_ready, lay * 5 + 5)
            key_of(0)
            for b in range(DEC_B):
                if b + 1 < DEC_B:
                    key_of(b + 1)
                dve.wait_ge(ss_done, lay * 8 + b + 1)
                if b >= 2:
                    dve.wait_ge(sn_out[b % 2], (lay * 4 + b // 2) * 16)
                for h in range(R_HEADS):
                    last = dve.scalar_tensor_tensor(
                        out=SN[:, b % 2, h, :], in0=S0[:, b % 2, h, :], scalar=G_STEP[h],
                        in1=PS[:, 2 + h // 2, (h % 2) * 256:(h % 2 + 1) * 256], op0=ALU.mult, op1=ALU.add)
                last.then_inc(sn_ready, 1)
            variances(4, 1)
            dve.wait_ge(ot_done, lay * 5 + 5)
            dve.tensor_copy(ROT[:, 1:8:2, SEQ:N], PS[:, 1, 0:P].rearrange("p (h c) -> p h c", c=NS)).then_inc(ot_dve, 1)

            def done(tile):
                dve.wait_ge(tile_done, lay * NT + tile + 1)

            def scaled(tile, p, dst):
                done(tile)
                dve.tensor_tensor(halves(dst), pair[p], RB, ALU.mult).then_inc(tile_free, 1)

            hold(dve, ot_act, lay * 5 + 5)
            dve.wait_ge(ot_dve, lay * 5 + 5)
            dve.wait_ge(st_out, lay * 16 + 16)
            for b in range(2):
                hold(dve, sn_out[b], lay * 64 + 64)
            with own.loop(2, 4) as i:
                for j in range(2):
                    ahead("rg", i, j)
                    for m in range(2):
                        k = 4 * i + (2 * j + m)
                        scaled(k + T0["rg"], m, EA[:, m, :])
                        dve.wait_ge(sig_done, lay * NSIG + k + (S0N["rg"] + 1))
                        own.mark(dve.tensor_tensor(EA[:, m, :], EA[:, m, :], EB[:, m, :], ALU.mult))
                        own.wait()
                        dve.tensor_tensor(EA[:, m:m + 1, :], EA[:, m:m + 1, :], ROT[:, bass.ds(k, 1), :],
                                          ALU.mult).then_inc(val_ready, 1)
                        dve.wait_ge(hi_val, lay * NX + k + (X0["rg"] + 1))
                        dve.tensor_tensor(ROL[:, bass.ds(k, 1), :], EA[:, m:m + 1, :],
                                          ROH[:, bass.ds(k, 1), :].bitcast(F32), ALU.subtract).then_inc(x_lo, 1)
            with own.loop(4, 0) as i:
                for j in range(2):
                    ahead("br_ret", i, j)
                    for m in range(2):
                        tile = 4 * i + (T0["br_ret"] + 2 * j + m)
                        if j == 0:
                            scaled(tile, m, EA[:, m, :])
                        else:
                            dve.wait_ge(sig_done, lay * NSIG + 2 * i + (S0N["br_ret"] + m + 1))
                            done(tile)
                            dve.tensor_tensor(G1[:, bass.ds(2 * i + m, 1), :].rearrange("p o (h c) -> p (o h) c", h=2),
                                              pair[m], halves(EB[:, m, :]), ALU.mult).then_inc(tile_free, 1)
            with own.loop(4, 0) as i:
                for j in range(2):
                    ahead("br_att", i, j, 4 * UC if j == 0 else 8 * UC)
                    for m in range(2):
                        tile = 4 * i + (T0["br_att"] + 2 * j + m)
                        if j == 0:
                            scaled(tile, m, EA[:, m, :])
                        else:
                            dve.wait_ge(sig_done, lay * NSIG + 2 * i + (S0N["br_att"] + m + 1))
                            done(tile)
                            dve.tensor_tensor(halves(EA[:, m, :]), pair[m], halves(EB[:, m, :]), ALU.mult)\
                                .then_inc(tile_free, 1)
                            dve.wait_ge(tile_free, lay * NT + tile + 3)
                            k = bass.ds(2 * i + m, 1)
                            dve.tensor_tensor(G1[:, k, :], G1[:, k, :], EA[:, m:m + 1, :], ALU.add).then_inc(val_ready, 1)
                            dve.wait_ge(hi_val, lay * NX + 2 * i + (X0["br_att"] + m + 1))
                            dve.tensor_tensor(ROL[:, k, :], G1[:, k, :], ROH[:, k, :].bitcast(F32),
                                              ALU.subtract).then_inc(x_lo, 1)

            def residual(tile, p, k, gcol, hi, squared):
                done(tile)
                x = XT[:, bass.ds(k, 1), :]
                v = x.rearrange("p o (h c) -> p (o h) c", h=2)
                dve.tensor_tensor(v, v, pair[p], ALU.add).then_inc(tile_free, 1)
                dve.wait_ge(tile_free, lay * NT + tile + 3)
                low_x(bass.ds(k, 1), bass.ds(gcol, 1), hi, squared)

            own.mark(dve.memset(EB[:, 1, :], 0.0))
            own.hold()
            with own.loop(2, 0) as i:
                for j in range(2):
                    ahead("out", i, j)
                    for m in range(2):
                        k = 4 * i + (2 * j + m)
                        residual(k + T0["out"], m, k, 8 * lay + k + 16, lay * NX + k + (X0["out"] + 1),
                                 (2 * lay + 1) * KT + k)
            norm(2 * lay + 2)
            own.hold()

            with own.loop(FT // 2, 2) as i:
                for j in range(2):
                    ahead("gu", i, j)
                    tile = 4 * i + (2 * j + T0["gu"])
                    f = 2 * i + j
                    scaled(tile, 0, EA[:, 0, :])
                    dve.wait_ge(sig_done, lay * NSIG + f + (S0N["gu"] + 1))
                    own.mark(dve.tensor_tensor(EB[:, 0, :], EB[:, 0, :], EA[:, 0, :], ALU.mult))
                    scaled(tile + 1, 1, EA[:, 1, :])
                    own.wait()
                    dve.wait_ge(tile_free, lay * NT + tile + 4)
                    dve.tensor_tensor(EA[:, 1, :], EA[:, 1, :], EB[:, 0, :], ALU.mult).then_inc(val_ready, 1)
                    dve.wait_ge(hi_val, lay * NX + f + (X0["gu"] + 1))
                    dve.tensor_tensor(AL[:, bass.ds(f, 1), :], EA[:, 1:2, :], AH[:, bass.ds(f, 1), :].bitcast(F32),
                                      ALU.subtract).then_inc(x_lo, 1)

            def down(i, m, last=False):
                k = 2 * i + m
                split(4 * i + (U0["down"] + 2 * m + 1), 1, 11 * P)
                if not last:
                    split(4 * i + (U0["down"] + 2 * m + 2), 0, 8 * UC)
                residual(k + T0["down"], m, k, 24 * lay + k + 8, lay * NX + k + (X0["down"] + 1),
                         (2 * lay + 2) * KT + k)

            own.mark(dve.memset(EB[:, 1, :], 0.0))
            own.hold()
            with own.loop(KT // 2 - 1, 0) as i:
                for m in range(2):
                    down(i, m)
            down(KT // 2 - 1, 0)
            down(KT // 2 - 1, 1, True)
            norm(2 * lay + 3)
            assert own.n == LAYER_MARKS, f"marks of a layer: {own.n}"
        own.base, own.n = 0, start + DEPTH * LAYER_MARKS

        dve.tensor_tensor(XT[:], XT[:], GT[:, 32:40].unsqueeze(2).to_broadcast([P, KT, N]), ALU.mult)\
           .then_inc(xg_ready, 1)

    ctx.close()


LAYER_MARKS = 192


def kernel(**inputs):
    import concourse.bacc as bacc
    from concourse.bass_utils import run_bass_kernel_spmd

    nc = bacc.Bacc("TRN2", target_bir_lowering=False, num_devices=1)
    names = ["x_prompt", "x_sample", "cache_k", "cache_v", "state_ret", "page_table", "g_mix", "w_in", "w_br_ret",
             "w_br_att", "w_out", "g_ffn", "w_gu", "w_down", "g_final"]
    data = {n: np.ascontiguousarray(inputs[n]) for n in names}
    data["consts_layer"], data["consts_fixed"] = shape_constants()
    arrays = {f"in_{n}": a for n, a in data.items()}
    args = [nc.dram_tensor(f"in_{n}", a.shape, mybir.dt.from_np(a.dtype), kind="ExternalInput").ap()
            for n, a in data.items()]
    outs = [(1, SEQ, D_MODEL), (DEC_B, DEC_L, D_MODEL), (DEPTH, 1, SEQ, M_HEADS, M_DH), (DEPTH, 1, SEQ, M_HEADS, M_DH),
            (DEPTH, 1, R_HEADS, R_DK, R_DV), (DEPTH, DEC_B, DEC_L, M_HEADS, M_DH),
            (DEPTH, DEC_B, DEC_L, M_HEADS, M_DH), (DEPTH, DEC_B, R_HEADS, R_DK, R_DV)]
    args += [nc.dram_tensor(f"out_{i}", s, F32, kind="ExternalOutput").ap() for i, s in enumerate(outs)]
    build(nc, *args)
    r = run_bass_kernel_spmd(nc, [arrays], core_ids=[0])
    return tuple(r.results[0][f"out_{i}"] for i in range(len(outs)))
```

```python
from contextlib import ExitStack, contextmanager

import numpy as np

import concourse.bass as bass
from concourse import mybir

F32 = mybir.dt.float32
F32R = mybir.dt.float32r
I32 = mybir.dt.int32
ALU = mybir.AluOpType
ACT = mybir.ActivationFunctionType
AX = mybir.AxisListType.X

P = 128
D_MODEL, SEQ, DEPTH = 1024, 512, 2
DEC_B, DEC_L, PAST, PAGE = 8, 4, 1024, 128
R_HEADS, R_DK, R_DV = 4, 128, 256
M_HEADS, M_DH, M_BLOCK = 8, 64, 256
D_FF = 2816
EPS = 1e-6
NS = DEC_B * DEC_L
N = SEQ + NS
HALF = N // 2
KT = D_MODEL // P
FT = D_FF // P
TT = SEQ // P + 1
ROWS = [P] * (TT - 1) + [NS]
UC = 256
N_PAGES = PAST // PAGE
GRP = 4
NG = DEC_B // GRP
V_STEP = NG * N_PAGES
BIG = 1e30
M_SCALE = M_DH ** -0.5
LOG_G = np.log1p(-np.exp2(-5.0 - np.arange(R_HEADS, dtype=np.float32))).astype(np.float32)
G_CHUNK = [float(x) for x in np.exp(LOG_G * np.float32(P))]
G_STEP = [float(x) for x in np.exp(LOG_G * np.float32(DEC_L))]

PHASES = [("mqk", 4, 20), ("mv", 2, 10), ("rqk", 4, 20), ("rv", 4, 20), ("rg", 4, 8), ("br_ret", 8, 16),
          ("br_att", 8, 16), ("out", 4, 8), ("gu", 22, 44), ("down", 16, 8)]
U0, T0, _u, _t = {}, {}, 0, 1
for _n, _a, _b in PHASES:
    U0[_n], T0[_n] = _u, _t
    _u, _t = _u + _a, _t + _b
NU, NT = _u, _t - 1
NX = 4 * KT + FT
X0 = {"rg": KT, "br_att": 2 * KT, "out": 3 * KT, "gu": 4 * KT, "down": 4 * KT + FT}
S0N = {"rg": 0, "br_ret": KT, "br_att": 2 * KT, "gu": 3 * KT}
V0N = {"rg": 0, "br_att": KT, "gu": 2 * KT}
NSIG, NVAL = 3 * KT + FT, 2 * KT + FT
C_MQ, C_MV, C_RQ, C_RV, C_RG, C_GR, C_GA = 3072, 4096, 0, 1024, 2048, 4608, 5632

CA_PARTS = [("causal", P), ("dect", 4 * P), ("qdt", 4 * P), ("cosr", TT * 64), ("sinr", TT * 64),
            ("cosm", TT * 32), ("sinm", TT * 32), ("kdec", 4), ("kdecs", 4), ("own", NG * NS), ("headm", 8),
            ("sel", 16), ("seqm", 8), ("qds", 128), ("decs", 128), ("rank", 4)]
CA, _c = {}, 0
for _n, _w in CA_PARTS:
    CA[_n] = (_c, _w)
    _c += _w
NCA = _c


def shape_constants():
    f = np.float32
    t = np.zeros((P, NCA), f)

    def put(name, a):
        a = np.asarray(a, f)
        t[:a.shape[0], CA[name][0]:CA[name][0] + CA[name][1]] = a.reshape(a.shape[0], -1)

    pos = np.zeros((P, TT), f)
    for i in range(TT - 1):
        pos[:, i] = i * P + np.arange(P)
    pos[:NS, TT - 1] = PAST + np.arange(NS) % DEC_L
    fr = (f(1.0) / np.power(f(10000.0), np.linspace(0.0, 1.0, R_DK // 2, dtype=f))).astype(f)
    fm = np.power(f(10000.0), (-np.arange(32, dtype=f) / f(32))).astype(f)
    for fq, c, s in ((fr, "cosr", "sinr"), (fm, "cosm", "sinm")):
        a = (pos[:, :, None] * fq[None, None, :]).astype(f).astype(np.float64)
        put(c, np.cos(a))
        put(s, np.sin(a))
    i, j = np.arange(P)[None, :], np.arange(P)[:, None]
    put("causal", np.where(j >= i, 0.0, -BIG))
    lg = LOG_G
    diff = (i - j).astype(f)
    put("dect", np.stack([np.where(diff >= 0, np.exp(g * np.maximum(diff, 0)), 0) for g in lg], 1))
    put("qdt", np.broadcast_to(np.exp(lg[:, None] * (np.arange(P, dtype=f)[None] + 1))[None], (P, 4, P)))
    put("kdec", np.exp(lg[None, :] * (P - 1.0 - np.arange(P, dtype=f)[:, None])))
    b, q = np.arange(NS) // DEC_L, (np.arange(NS) % DEC_L).astype(f)
    put("kdecs", np.exp(lg[None, :] * (DEC_L - 1.0 - q[:, None])))
    put("qds", np.broadcast_to(np.exp(lg[:, None] * (q[None] + 1))[None], (P, 4, NS)))
    same = b[:, None] == b[None, :]
    ds = q[None, :] - q[:, None]
    put("decs", np.stack([np.where(same & (ds >= 0), np.exp(g * np.maximum(ds, 0)), 0) for g in lg], 1))
    put("seqm", b[:, None] == np.arange(DEC_B)[None])
    r = np.arange(P)
    rb, rh, rq = r // 32, (r % 32) // 4, r % 4
    put("own", np.stack([np.where((b[None] == (g * GRP + rb)[:, None]) & (q[None] <= rq[:, None]), 0.0, -BIG)
                         for g in range(NG)], 1))
    put("headm", rh[:, None] == np.arange(8)[None])
    put("sel", (rb * 4 + rq)[:, None] == np.arange(16)[None])
    put("rank", np.broadcast_to(np.arange(1, 5, dtype=f), (P, 4)))
    return t, np.concatenate([np.eye(P, dtype=f), np.ones((P, P), f)], 1)


class Order:

    def __init__(self, eng, sem):
        self.eng, self.sem, self.base, self.n = eng, sem, 0, 0

    def mark(self, ins):
        ins.then_inc(self.sem, 1)
        self.n += 1

    def wait(self):
        self.eng.wait_ge(self.sem, self.base + self.n)

    def hold(self):
        hold(self.eng, self.sem, self.base + self.n)

    @contextmanager
    def loop(self, count, each):
        base, n = self.base, self.n
        with self.eng.Fori(0, count) as i:
            self.base, self.n = base + n + i * each, 0
            yield i
            assert self.n == each, f"marks in the loop: {self.n}, not {each}"
        self.base, self.n = base, n + count * each


IDLE = []


def hold(eng, sem, value):
    if isinstance(value, int):
        return eng.wait_ge(sem, value)
    with eng.register() as count:
        eng.reg_mov(count, value)
        eng.wait_ge(IDLE[0], 0)
        eng.wait_ge(sem, count)


def wait(eng, sem, value):
    eng.wait_ge(sem, value)


def build(nc, x_prompt, x_sample, cache_k, cache_v, state_ret, page_table, g_mix, w_in, w_br_ret, w_br_att,
          w_out, g_ffn, w_gu, w_down, g_final, consts_layer, consts_fixed,
          y_prompt, y_sample, k_prompt, v_prompt, state_prompt, k_sample, v_sample, state_sample):
    ctx = ExitStack()
    top = [16512]

    def at(name, shape, dt=F32, off=None):
        size = 4 * int(np.prod(shape[1:]))
        if off is None:
            off, top[0] = top[0], top[0] + (size + 31) // 32 * 32
        assert off + size <= 229344, (name, off + size)
        return nc.alloc_sbuf_tensor_at(name, shape, dt, offset=off)

    def sem(name):
        return ctx.enter_context(nc.semaphore(name))

    XT = at("XT", [P, KT, N])
    XH, XL = at("XH", [P, KT, N], F32R), at("XL", [P, KT, N], F32R)
    RAW = at("RAW", [P, 2, 8 * UC])
    WH, WL = at("WH", [P, 2, 8 * UC], F32R), at("WL", [P, 2, 8 * UC], F32R)
    FIX = at("FIX", [P, 2 * P])
    IDENT, ONES = FIX[:, 0:P], FIX[:, P:2 * P]
    GT = at("GT", [P, 40])
    RSTDB = at("RSTDB", [P, N])
    EAOFF = top[0]
    EA = at("EA", [P, 2, N])
    EB = at("EB", [P, 2, N])
    SM = at("SM", [P, 96])
    RT, RTK, VAR = SM[:, 0:5], SM[:, 5:10], SM[:, 10:15]
    MX, NM, RSUM, RINV = SM[:, 16:20], SM[:, 20:24], SM[:, 36:40], SM[:, 92:96]
    SSQ, RMS, RRS = SM[:, 24:28], SM[:, 28:32], SM[:, 32:36]
    BS, BM, PEN, BIAS, EQ = SM[:, 40:44], SM[:, 44:49], SM[:, 50:54], SM[:, 54:59], SM[:, 60:64]
    T1A, ES, SRI, MHALF = SM[:, 64:66], SM[:, 68:73], SM[:, 74:76], SM[:, 80:85]
    PTAB = at("PTAB", [1, DEC_B * N_PAGES], I32)
    XS = EA[:, 0, 0:512].rearrange("p (a c) -> p a c", a=2)
    RO1, RO2 = EA[:, 1, 0:256], EA[:, 1, 256:512]
    IND, QD = EA[:, 0, 0:512], EA[:, 1, 0:512]
    DIAG = EA[:].rearrange("p a n -> p (a n)")[:, 0:TT * P].rearrange("p (t c) -> p t c", t=TT)

    R0 = top[0]
    AH, AL = at("AH", [P, FT, N], F32R, R0), at("AL", [P, FT, N], F32R, R0 + FT * N * 4)
    CL = at("CL", [P, NCA], F32, R0)
    R1 = R0 + NCA * 4 + 32 & ~31
    MOH, MOL = at("MOH", [P, 4, N], F32R, R1), at("MOL", [P, 4, N], F32R, R1 + 16 * N)
    GREG = R1 + 32 * N
    G1 = at("G1", [P, KT, N], F32, GREG)
    ROREG = GREG + 4 * KT * N
    ROH, ROL = at("ROH", [P, KT, N], F32R, ROREG), at("ROL", [P, KT, N], F32R, ROREG + 4 * KT * N)
    o = GREG
    MT = at("MT", [P, 8, N], F32, o); o += 32 * N
    MV = at("MV", [P, TT, 512], F32, o); o += TT * 2048
    PG = at("PG", [P, 2, GRP, 512], F32, o); o += GRP * 4096
    QK = at("QK", [P, TT, 1024], F32, o)
    PR = at("PR", [P, 4, 512], F32, o)
    PT = at("PT", [P, 2, 4, 512], F32, o + 8192)
    KTT = [at("KTT0", [P, GRP, 4, P], F32, o), at("KTT1", [P, GRP, 4, P], F32, EAOFF)]; o += GRP * 2048
    SP_ = at("SP_", [P, 2, PAST + NS], F32, o); o += 8 * (PAST + NS)
    PTS = at("PTS", [P, 9, P], F32, o); o += 9 * 512
    QB = at("QB", [P, 4, 256], F32, o); o += 4096
    OS = at("OS", [P, 512], F32, o)
    RQ = at("RQ", [P, TT, 512], F32, GREG)
    ROT = G1
    o = ROREG
    RTT = at("RTT", [P, 8, N], F32, o); o += 32 * N
    RK = at("RK", [P, TT, 512], F32, o)
    QM = at("QM", [P, 4, 256], F32, o)
    KM = at("KM", [P, 2, 512], F32, o + 4096); o += TT * 2048
    RV = at("RV", [P, TT, 1024], F32, o)
    S0 = at("S0", [P, 4, 4, 256], F32, o); o += TT * 4096
    ST = at("ST", [P, 4, 256], F32, o)
    SGATE = at("SGATE", [P, KT, NS], F32, o + 4096)
    XIN = at("XIN", [P, TT, D_MODEL], F32, GREG)
    GIN = at("GIN", [40, P], F32, GREG + TT * 4096)
    YO = at("YO", [P, 2, D_MODEL], F32, GREG)

    PS = ctx.enter_context(nc.psum_tensor("PS", [P, 8, 512], F32))

    def cl(name, rows=P):
        a, w = CA[name]
        return CL[0:rows, a:a + w]

    IDLE[:] = [sem("idle")]
    consts_in, x_in, g_in, ptab_in = sem("consts_in"), sem("x_in"), sem("g_in"), sem("ptab_in")
    cl_in = sem("cl_in")
    landed = [sem("landed0"), sem("landed1")]
    hi_ready, lo_ready, half_done = sem("hi_ready"), sem("lo_ready"), sem("half_done")
    tile_done, tile_free = sem("tile_done"), sem("tile_free")
    rot_free = sem("rot_free")
    dve_own, act_own = sem("dve_own"), sem("act_own")
    xt_done, xt_copied, g_ready, x_lo = sem("xt_done"), sem("xt_copied"), sem("g_ready"), sem("x_lo")
    sq_added, nsum, nvar, nrt, ndiag, nbc = (sem(s) for s in ("sq_added", "nsum", "nvar", "nrt", "ndiag", "nbc"))
    rt_ready, rt_taken = sem("rt_ready"), sem("rt_taken")
    xg_ready, mhalf_set = sem("xg_ready"), sem("mhalf_set")
    tr_done, tr_act, tr_dve = sem("tr_done"), sem("tr_act"), sem("tr_dve")
    s_done, s_max, s_exp, s_prob = sem("s_done"), sem("s_max"), sem("s_exp"), sem("s_prob")
    pt_done, pt_evac, pv_done, mo_hi, mo_lo = (sem(s) for s in ("pt_done", "pt_evac", "pv_done", "mo_hi", "mo_lo"))
    page_in = [sem(f"page_in{i}") for i in range(3)]
    page_in_b = [sem(f"page_in_b{i}") for i in range(3)]
    qb_ready, kt_done, kt_act, kt_dve, sc_done = (sem(s) for s in ("qb_ready", "kt_done", "kt_act", "kt_dve", "sc_done"))
    sel_ready, e_done, pts_done, pts_act, pts_dve = (sem(s) for s in ("sel_ready", "e_done", "pts_done", "pts_act", "pts_dve"))
    pvs_page, os_ready, mos_done, mos_hi, mos_lo = (sem(s) for s in ("pvs_page", "os_ready", "mos_done", "mos_hi", "mos_lo"))
    kv_out, st_out, y_out = sem("kv_out"), sem("st_out"), sem("y_out")
    kd_ready, in_done, in_masked, o_done, st_done, st_ready = (
        sem(s) for s in ("kd_ready", "in_done", "in_masked", "o_done", "st_done", "st_ready"))
    ssq_ready, var_ready, rms_ready, o_scaled, ot_done, ot_act, ot_dve = (
        sem(s) for s in ("ssq_ready", "var_ready", "rms_ready", "o_scaled", "ot_done", "ot_act", "ot_dve"))
    s0_in = [sem(f"s0_in{i}") for i in range(4)]
    sn_out = [sem(f"sn_out{i}") for i in range(4)]
    qm_ready, km_ready, ss_done, sn_ready, so_done = (sem(s) for s in ("qm_ready", "km_ready", "ss_done", "sn_ready", "so_done"))
    hi_rot, rot_gated = sem("hi_rot"), sem("rot_gated")
    sig_done, val_ready, hi_val = sem("sig_done"), sem("val_ready"), sem("hi_val")

    block = ctx.enter_context(nc.Block())

    def diag(t, row):
        a = t[:, 0, 0:4]
        return bass.AP(a.tensor, a.offset + 0, [list(a.ap[0]), [256, 4], [36, 8], [1, 4]])

    def page_slot(r):
        if r < V_STEP:
            used = [r % 2 == q % 2 for q in range(r)]
            return r % 2, PG[:, r % 2], sum(used), V_STEP // 2 + len(range(r % 2, V_STEP, 3))
        slot, before = (r - V_STEP) % 3, (r - V_STEP) // 3
        keys = V_STEP // 2 if slot < 2 else 0
        buf = PG[:, slot] if slot < 2 else KTT[0][:].rearrange("p b k c -> p b (k c)")
        return slot, buf, keys + before, keys + len(range(slot, V_STEP, 3))

    def pages(eng, lay, seqs, arrived, between=None):
        for r in range(4 * N_PAGES):
            if between is not None:
                between(r)
            slot, buf, _, _ = page_slot(r)
            for b in seqs:
                if r >= V_STEP + 3:
                    hold(eng, pvs_page, lay * 64 + 4 * (r - V_STEP - 3) + b + 1)
                elif r >= V_STEP + 2:
                    hold(eng, sc_done, lay * 18 + 18)
                elif r >= 2:
                    hold(eng, kt_done, lay * 64 + 4 * (r - 2) + b + 1)
                e = (r // N_PAGES % 2 * GRP + b) * N_PAGES + r % N_PAGES
                page = eng.value_load(PTAB[0:1, e:e + 1], min_val=0, max_val=cache_k.shape[1] - 1)
                src = (cache_k, cache_v)[r // (2 * N_PAGES)][bass.ds(lay, 1), bass.ds(page, 1)]
                eng.dma_start(buf[:, b, :], src.rearrange("o n p h d -> p (o n h d)")).then_inc(arrived[slot], 16)

    @block.sync
    def _(sp):
        sp.dma_start(PTAB[:], page_table.rearrange("b n -> (b n)").unsqueeze(0)).then_inc(ptab_in, 16)
        sp.dma_start(FIX[:], consts_fixed).then_inc(consts_in, 16)
        sp.dma_start(XIN[:, 0:TT - 1, :], x_prompt[0].rearrange("(t p) d -> p t d", p=P)).then_inc(x_in, 16)
        sp.dma_start(XIN[0:NS, TT - 1, :], x_sample.rearrange("b l d -> (b l) d")).then_inc(x_in, 16)
        sp.dma_start(GIN[0:16, :], g_mix.rearrange("l (m p) -> (l m) p", p=P)).then_inc(g_in, 16)
        sp.dma_start(GIN[16:32, :], g_ffn.rearrange("l (m p) -> (l m) p", p=P)).then_inc(g_in, 16)
        sp.dma_start(GIN[32:40, :], g_final.rearrange("(m p) -> m p", p=P)).then_inc(g_in, 16)
        sp.wait_ge(ptab_in, 16)
        with sp.Fori(0, DEPTH) as lay:
            def unit(u, slot, parts):
                (hold if isinstance(u, int) else wait)(sp, lo_ready, lay * NU + u + 1)
                for dst, src in parts:
                    sp.dma_start(dst, src).then_inc(landed[slot], 16)

            def rows(w, k0, k):
                return w[bass.ds(lay, 1), k0 * P:(k0 + k) * P, :].rearrange("o (k p) c -> p (o k) c", p=P)

            def full(u, slot, w, k, col):
                dst = RAW[:, slot, 0:k * UC].rearrange("p (k c) -> p k c", c=UC)
                h = k // 2
                unit(u, slot, [(dst[:, 0:h], rows(w, 0, h)[:, :, bass.ds(col, UC)]),
                               (dst[:, h:k], rows(w, h, h)[:, :, bass.ds(col, UC)])])

            def run(name, w, col, count, skip=0):
                with sp.Fori(0, count) as i:
                    for j in range(2):
                        full(U0[name] + skip + 2 * i + j, j, w, KT, col + (2 * i + j) * UC)

            for j in range(2):
                full(U0["mqk"] + j, j, w_in, KT, C_MQ + j * UC)
            hold(sp, tile_done, lay * NT + 1)
            sp.dma_start(CL[:], consts_layer).then_inc(cl_in, 16)
            for j in range(2):
                full(U0["mqk"] + 2 + j, j, w_in, KT, C_MQ + (2 + j) * UC)
            run("mv", w_in, C_MV, 1)
            for j in range(2):
                full(U0["rqk"] + j, j, w_in, KT, C_RQ + j * UC)

            def next_unit(r):
                if r in (V_STEP + 6, V_STEP + 10):
                    j = 2 + (r > V_STEP + 6)
                    full(U0["rqk"] + j, j % 2, w_in, KT, C_RQ + j * UC)

            pages(sp, lay, (0, 1), page_in, next_unit)
            run("rv", w_in, C_RV, 2)
            run("rg", w_in, C_RG, 2)
            with sp.Fori(0, 4) as i:
                full(U0["br_ret"] + 2 * i, 0, w_in, KT, C_GR + i * UC)
                full(U0["br_ret"] + 2 * i + 1, 1, w_br_ret, KT, i * UC)
            with sp.Fori(0, 4) as i:
                full(U0["br_att"] + 2 * i, 0, w_in, KT, C_GA + i * UC)
                full(U0["br_att"] + 2 * i + 1, 1, w_br_att, 4, i * UC)
            run("out", w_out, 0, 2)
            with sp.Fori(0, FT // 2) as i:
                for j in range(2):
                    dst = RAW[:, j, :].rearrange("p (k c) -> p k c", c=UC)
                    src = rows(w_gu, 0, KT)
                    col = (2 * i + j) * P
                    unit(U0["gu"] + 2 * i + j, j, [(dst[:, :, 0:P], src[:, :, bass.ds(col, P)]),
                                                   (dst[:, :, P:UC], src[:, :, bass.ds(col + D_FF, P)])])
            with sp.Fori(0, KT) as m:
                for j in range(2):
                    dst = RAW[:, j, 0:11 * P].rearrange("p (k c) -> p k c", c=P)
                    src = rows(w_down, 11 * j, 11)[:, :, bass.ds(m * P, P)]
                    unit(U0["down"] + 2 * m + j, j, [(dst[:, 0:6], src[:, 0:6]), (dst[:, 6:11], src[:, 6:11])])
        sp.wait_ge(lo_ready, DEPTH * NU + 1)
        for h in range(2):
            sp.dma_start(RAW[:, 0, h * 4 * UC:(h + 1) * 4 * UC].rearrange("p (k c) -> p k c", c=UC),
                         w_in[0, h * 4 * P:(h + 1) * 4 * P, 0:UC].rearrange("(k p) c -> p k c", p=P))\
                .then_inc(landed[0], 16)
        for t in range(TT):
            sp.wait_ge(o_scaled, DEPTH * 5 + t + 1)
            n = ROWS[t]
            dst = y_prompt[0, t * P:(t + 1) * P, :] if t < TT - 1 else y_sample.rearrange("b l d -> (b l) d")
            sp.dma_start(dst, YO[0:n, t % 2, :]).then_inc(y_out, 16)
            if t < TT - 2:
                sp.wait_ge(y_out, 16 * (t + 1))
        sp.wait_ge(y_out, 16 * TT)

    @block.gpsimd
    def _(pool):
        pool.memset(MHALF, -0.5).then_inc(mhalf_set, 1)
        pool.wait_ge(mhalf_set, 1)
        pool.memset(SM[:, 89:90], 0.0).then_inc(tile_done, 1)
        pool.memset(SM[:, 87:88], 0.0).then_inc(tile_free, 3)
        pool.memset(SM[:, 88:89], 0.0).then_inc(rot_free, 2)

        def norm(count):
            hold(pool, nvar, count)
            pool.tensor_tensor(RT, VAR, MHALF, ALU.pow).then_inc(nrt, 1)

        norm(1)
        pool.wait_ge(ptab_in, 16)
        with pool.Fori(0, DEPTH) as lay:
            hold(pool, rot_free, lay * 40 + 22)
            pool.dma_start(k_prompt[bass.ds(lay, 1)].rearrange("o b (t p) h d -> p (o b t) (h d)", p=P),
                           QK[:, 0:TT - 1, 512:1024]).then_inc(kv_out, 16)
            pool.dma_start(k_sample[bass.ds(lay, 1)].rearrange("o b l h d -> (o b l) (h d)"),
                           QK[0:NS, TT - 1, 512:1024]).then_inc(kv_out, 16)
            hold(pool, tile_free, lay * NT + T0["rqk"] + 2)
            pool.dma_start(v_prompt[bass.ds(lay, 1)].rearrange("o b (t p) h d -> p (o b t) (h d)", p=P),
                           MV[:, 0:TT - 1, :]).then_inc(kv_out, 16)
            pool.dma_start(v_sample[bass.ds(lay, 1)].rearrange("o b l h d -> (o b l) (h d)"),
                           MV[0:NS, TT - 1, :]).then_inc(kv_out, 16)
            pages(pool, lay, (2, 3), page_in_b)
            def load_state(b):
                pool.dma_start(S0[:, b % 4], state_ret[bass.ds(lay, 1), b].rearrange("o h k v -> k (o h) v"))\
                    .then_inc(s0_in[b % 4], 16)

            for c in range(TT):
                if c == TT - 1:
                    hold(pool, ot_done, lay * 5 + 4)
                    load_state(3)
                    hold(pool, st_ready, lay * 4 + 4)
                    pool.dma_start(state_prompt[bass.ds(lay, 1)].rearrange("o b h k v -> k (o b h) v"), ST[:])\
                        .then_inc(st_out, 16)
                    for b in range(DEC_B):
                        hold(pool, sn_ready, lay * 8 + b + 1)
                        pool.dma_start(state_sample[bass.ds(lay, 1), b].rearrange("o h k v -> k (o h) v"),
                                       S0[:, b % 4]).then_inc(sn_out[b % 4], 16)
                        if 1 <= b < 5:
                            hold(pool, sn_out[b - 1], lay * 32 + 16)
                            load_state(b + 3)
                hold(pool, var_ready, lay * 5 + c + 1)
                w = 4 if c < TT - 1 else 1
                pool.tensor_tensor(RRS[:, 0:w], RMS[:, 0:w], MHALF[:, 0:w], ALU.pow).then_inc(rms_ready, 1)
                if 1 <= c < TT - 1:
                    hold(pool, ot_done, lay * 5 + c)
                    load_state(c - 1)
            norm(2 * lay + 2)
            norm(2 * lay + 3)
        hold(pool, kv_out, DEPTH * 64)
        hold(pool, st_out, DEPTH * 16)
        for b in range(4):
            hold(pool, sn_out[b], DEPTH * 32)

    @block.tensor
    def _(pe):
        def square_sums(count):
            pe.wait_ge(sq_added, 8 * count)
            for t, n in enumerate(ROWS):
                last = pe.matmul(PS[0:n, 4, t:t + 1], EB[:, 1, t * P:t * P + n], ONES[:, 0:1], start=True, stop=True)
            last.then_inc(nsum, 1)

        def spread(count, banks):
            pe.wait_ge(ndiag, count)
            for t in range(TT - 1):
                pe.matmul(PS[:, banks[0], t * P:(t + 1) * P], ONES, DIAG[:, t, :], start=True, stop=True)
            pe.matmul(PS[:, banks[1], 0:NS], ONES[0:NS, :], DIAG[0:NS, TT - 1, 0:NS], start=True, stop=True)\
                .then_inc(nbc, 1)

        pe.wait_ge(consts_in, 16)
        pe.wait_ge(g_in, 48)
        pe.transpose(PS[:, 0, 0:40], GIN[:], IDENT[0:40, 0:40]).then_inc(xt_done, 1)
        pe.wait_ge(x_in, 32)
        for m in range(KT):
            if m >= 2:
                pe.wait_ge(xt_copied, m)
            for t, n in enumerate(ROWS):
                bank = 4 + 2 * (m % 2) + (t == TT - 1)
                dst = PS[:, bank, t * P:(t + 1) * P] if t < TT - 1 else PS[:, bank, 0:NS]
                last = pe.transpose(dst, XIN[0:n, t, m * P:(m + 1) * P], IDENT[0:n, 0:n])
            last.then_inc(xt_done, 1)

        x, kk = (XH, XL), list(range(KT))
        with pe.Fori(0, DEPTH) as lay:
            def split_ready(u):
                pe.wait_ge(lo_ready, lay * NU + u + 1 + 2)

            def token_tiles(u, slot, n0, x_at=None, only=None, banks=(0, 2)):
                split_ready(u)
                wh = WH[:, slot, :].rearrange("p (k c) -> p k c", c=UC)
                wl = WL[:, slot, :].rearrange("p (k c) -> p k c", c=UC)
                for t, n in enumerate(ROWS):
                    if only is not None and t != only:
                        continue
                    tile = n0 + t
                    bank = banks[(slot * TT + t) % 2]
                    pe.wait_ge(tile_free, lay * NT + tile + 1)
                    for k in range(KT):
                        if x_at is not None and t == 0 and k in (0, 6):
                            pe.wait_ge(x_lo, x_at - (2 if k == 0 else 0))
                        a, b = XH[:, k, t * P:t * P + n], XL[:, k, t * P:t * P + n]
                        pe.matmul(PS[0:n, bank, 0:UC], a, wh[:, k], start=k == 0, stop=False)
                        pe.matmul(PS[0:n, bank, 0:UC], a, wl[:, k], start=False, stop=False)
                        last = pe.matmul(PS[0:n, bank, 0:UC], b, wh[:, k], start=False, stop=k == KT - 1)
                    last.then_inc(tile_done, 1)
                    if x_at is not None and t == 0:
                        square_sums(2 * lay + 1)

            def feature_tile(tile, pair, slot, cols, c0, kts, rhs, first=True, final=True, part=None,
                             depth=4):
                wh = WH[:, slot, 0:len(kts) * cols].rearrange("p (k c) -> p k c", c=cols)
                wl = WL[:, slot, 0:len(kts) * cols].rearrange("p (k c) -> p k c", c=cols)
                hi, lo = rhs
                if first:
                    pe.wait_ge(tile_free, lay * NT + tile + 3 - depth)
                for i, k in enumerate(kts):
                    if part is not None and k not in part:
                        continue
                    for a, w, x in ((0, wh, hi), (1, wh, lo), (2, wl, hi)):
                        for h in range(2):
                            last = pe.matmul(PS[:, 2 * pair + h, 0:HALF], w[:, i, c0:c0 + P],
                                             x[:, k, h * HALF:(h + 1) * HALF],
                                             start=first and i == 0 and a == 0,
                                             stop=final and i == len(kts) - 1 and a == 2)
                if final:
                    last.then_inc(tile_done, 1)
                return last

            def unit2_late(u, slot, tile, rhs, x_at):
                split_ready(u)
                kk = range(KT)
                pe.wait_ge(x_lo, x_at - 2)
                feature_tile(tile, 2 * slot, slot, UC, 0, kk, rhs, final=False, part=kk[:6])
                feature_tile(tile + 1, 2 * slot + 1, slot, UC, P, kk, rhs, final=False, part=kk[:6])
                pe.wait_ge(x_lo, x_at)
                feature_tile(tile, 2 * slot, slot, UC, 0, kk, rhs, first=False, part=kk[6:])
                feature_tile(tile + 1, 2 * slot + 1, slot, UC, P, kk, rhs, first=False, part=kk[6:])

            def unit2(u, slot, tile, kts, rhs):
                split_ready(u)
                feature_tile(tile, 2 * slot, slot, UC, 0, kts, rhs)
                feature_tile(tile + 1, 2 * slot + 1, slot, UC, P, kts, rhs)

            def transposes(srcs, base):
                for j, src in enumerate(srcs):
                    if j >= 2:
                        done = tr_act if j % 2 == 0 else tr_dve
                        pe.wait_ge(done, lay * 8 + base // 2 + j // 2)
                    for t, n in enumerate(ROWS):
                        bank = 4 + 2 * (j % 2) + (t == TT - 1)
                        dst = PS[:, bank, t * P:(t + 1) * P] if t < TT - 1 else PS[:, bank, 0:NS]
                        last = pe.transpose(dst, src[0:n, t], IDENT[0:n, 0:n])
                    last.then_inc(tr_done, 1)
                pe.wait_ge(tr_act, lay * 8 + base // 2 + 4)
                pe.wait_ge(tr_dve, lay * 8 + base // 2 + 4)

            token_tiles(0, 0, T0["mqk"], lay * NX + KT)
            token_tiles(1, 1, T0["mqk"] + TT)
            with pe.Fori(1, 3) as i:
                for j in range(2):
                    token_tiles(2 * i + j, j, T0["mqk"] + (2 * i + j) * TT)
            pe.wait_ge(rot_free, lay * 40 + 22)
            transposes([QK[:, :, j * P:(j + 1) * P] for j in range(8)], 0)
            pe.wait_ge(tile_free, lay * NT + T0["rqk"] + 2)

            spread(2 * lay + 1, (1, 7))

            def scores(n):
                h, t = divmod(n, 4)
                r = slice(64 * (h % 2), 64 * (h % 2) + 64)
                if n >= 4:
                    pe.wait_ge(s_exp, lay * 32 + n - 3)
                pe.matmul(PS[:, 2 + n % 4, 0:(t + 1) * P], MT[r, h // 2, t * P:(t + 1) * P],
                          MT[r, 4 + h // 2, 0:(t + 1) * P], start=True, stop=True).then_inc(s_done, 1)

            def attend(h, kt):
                hp = h // 2
                if kt == 0:
                    pe.wait_ge(pt_evac, lay * 32 + 4 * h + 4)
                    if h % 2 == 0 and hp >= 2:
                        pe.wait_ge(mo_lo, lay * 4 + hp - 1)
                last = pe.matmul(PS[64 * (h % 2):64 * (h % 2) + 64, 1 + 6 * (hp % 2), kt * P:SEQ],
                                 MV[:, kt, h * 64:(h + 1) * 64], PT[:, h % 2, kt, kt * P:SEQ],
                                 start=kt == 0, stop=kt == 3)
                if h % 2 and kt == 3:
                    last.then_inc(pv_done, 1)

            for n in range(3):
                scores(n)
            for n in range(32):
                h, t = divmod(n, 4)
                if n + 3 < 32:
                    scores(n + 3)
                pe.wait_ge(s_prob, lay * 32 + n + 1)
                if n >= 2:
                    pe.wait_ge(pt_evac, lay * 32 + n - 1)
                for kt in range(t + 1):
                    last = pe.transpose(PS[:, 6 * (1 - n % 2), kt * P:(kt + 1) * P],
                                        PR[:, n % 4, kt * P:(kt + 1) * P], IDENT)
                last.then_inc(pt_done, 1)
                if h:
                    attend(h - 1, t)
            for kt in range(4):
                attend(M_HEADS - 1, kt)

            def turn_keys(q):
                r = q
                slot, buf, before, per = page_slot(r)
                pe.wait_ge(page_in[slot], (lay * per + before + 1) * 32)
                pe.wait_ge(page_in_b[slot], (lay * per + before + 1) * 32)
                for b in range(GRP):
                    c = 4 * q + b
                    if c >= 3:
                        pe.wait_ge(kt_act if (c - 3) % 2 == 0 else kt_dve, lay * 32 + (c - 3) // 2 + 1)
                    for hp in range(4):
                        last = pe.transpose(PS[:, c % 3, hp * P:(hp + 1) * P],
                                            buf[:, b, hp * P:(hp + 1) * P], IDENT)
                    last.then_inc(kt_done, 1)

            def key_scores(q):
                g, p = q // 8, q % 8
                pe.wait_ge(kt_act, lay * 32 + 2 * q + 2)
                pe.wait_ge(kt_dve, lay * 32 + 2 * q + 2)
                for hp in range(4):
                    for b in range(GRP):
                        last = pe.matmul(PS[32 * b:32 * b + 32, 4 + 2 * g + p // 4, (p % 4) * P:(p % 4 + 1) * P],
                                         QB[:, hp, (g * GRP + b) * 32:(g * GRP + b + 1) * 32],
                                         KTT[q % 2][:, b, hp, :], start=hp == 0, stop=hp == 3)
                last.then_inc(sc_done, 1)
                if p == N_PAGES - 1:
                    for hp in range(4):
                        for b in range(GRP):
                            last = pe.matmul(PS[32 * b:32 * b + 32, 3, g * NS:(g + 1) * NS],
                                             QB[:, hp, (g * GRP + b) * 32:(g * GRP + b + 1) * 32],
                                             MT[:, 4 + hp, SEQ:N], start=hp == 0, stop=hp == 3)
                    last.then_inc(sc_done, 1)

            pe.wait_ge(mo_lo, lay * 4 + 4)
            turn_keys(0)
            pe.wait_ge(qb_ready, lay + 1)
            for q in range(NG * N_PAGES):
                if q + 1 < NG * N_PAGES:
                    turn_keys(q + 1)
                key_scores(q)
            def to_columns(g):
                pe.wait_ge(os_ready, lay * 2 + g + 1)
                for hp in range(4):
                    last = pe.matmul(PS[:, 3, 64 + g * 64 + hp * 16:64 + g * 64 + (hp + 1) * 16],
                                     OS[:, hp * P:(hp + 1) * P], cl("sel"), start=True, stop=True)
                last.then_inc(mos_done, 1)

            for g in range(NG):
                pe.wait_ge(e_done, lay * 2 + g + 1)
                for p in range(N_PAGES):
                    pe.transpose(PS[:, p // 4, (p % 4) * P:(p % 4 + 1) * P], SP_[:, g, p * P:(p + 1) * P], IDENT)
                pe.transpose(PS[0:NS, 2, 0:P], SP_[:, g, PAST:PAST + NS], IDENT).then_inc(pts_done, 1)
                pe.wait_ge(pts_act, lay * 2 + g + 1)
                pe.wait_ge(pts_dve, lay * 2 + g + 1)
                for p in range(N_PAGES):
                    r = V_STEP + g * 8 + p
                    slot, buf, before, per = page_slot(r)
                    pe.wait_ge(page_in[slot], (lay * per + before + 1) * 32)
                    pe.wait_ge(page_in_b[slot], (lay * per + before + 1) * 32)
                    for b in range(GRP):
                        last = pe.matmul(PS[32 * b:32 * b + 32, 4 + 2 * g, :], PTS[:, p, 32 * b:32 * b + 32],
                                         buf[:, b, :], start=p == 0, stop=False)
                        last.then_inc(pvs_page, 1)
                    if g and p == 0:
                        to_columns(0)
                    t = p - (3 if g == 0 else 0)
                    if 0 <= t < TT:
                        if g == t == 0:
                            pe.wait_ge(e_done, lay * 2 + 2)
                        token_tiles(U0["rqk"] + g, g, T0["rqk"] + g * TT, only=t, banks=(5, 7))
                for b in range(GRP):
                    last = pe.matmul(PS[32 * b:32 * b + 32, 4 + 2 * g, :], PTS[0:NS, 8, 32 * b:32 * b + 32],
                                     MV[0:NS, TT - 1, :], start=False, stop=True)
                last.then_inc(pts_done, 1)
            to_columns(1)
            hold(pe, mos_lo, lay * 2 + 2)

            with pe.Fori(1, 4) as i:
                for j in range(2):
                    token_tiles(U0["rqk"] + 2 * i + j, j, T0["rqk"] + (2 * i + j) * TT)
            pe.wait_ge(rot_free, lay * 40 + 42)
            transposes([RQ[:, :, j * P:(j + 1) * P] for j in range(4)]
                       + [RK[:, :, j * P:(j + 1) * P] for j in range(4)], 8)
            pe.wait_ge(tile_free, lay * NT + T0["rg"] + 2)

            def inner(c):
                if c:
                    pe.wait_ge(in_masked, lay * 5 + c)
                for h in range(R_HEADS):
                    last = pe.matmul(PS[:, 4, h * P:(h + 1) * P], RTT[:, 4 + h, c * P:(c + 1) * P],
                                     RTT[:, h, c * P:(c + 1) * P], start=True, stop=True)
                last.then_inc(in_done, 1)

            def chunk(c):
                pe.wait_ge(in_masked, lay * 5 + c + 1)
                if c:
                    pe.wait_ge(o_scaled, lay * 5 + c)
                    pe.wait_ge(st_ready, lay * 4 + c)
                for h in range(R_HEADS):
                    dst = PS[:, 5 + h // 2, (h % 2) * 256:(h % 2 + 1) * 256]
                    last = pe.matmul(dst, IND[:, h * P:(h + 1) * P], RV[:, c, h * 256:(h + 1) * 256],
                                     start=True, stop=c == 0)
                    if c:
                        last = pe.matmul(dst, QD[:, h * P:(h + 1) * P], ST[:, h, :], start=False, stop=True)
                last.then_inc(o_done, 1)
                pe.wait_ge(kd_ready, lay * 5 + c + 1)
                for h in range(R_HEADS):
                    last = pe.matmul(PS[:, 2 + h // 2, (h % 2) * 256:(h % 2 + 1) * 256],
                                     RK[:, c, h * P:(h + 1) * P], RV[:, c, h * 256:(h + 1) * 256],
                                     start=True, stop=True)
                last.then_inc(st_done, 1)

            def turn(c):
                pe.wait_ge(o_scaled, lay * 5 + c + 1)
                if c:
                    pe.wait_ge(ot_act, lay * 5 + c)
                    pe.wait_ge(ot_dve, lay * 5 + c)
                for j in range(8):
                    last = pe.transpose(PS[:, j // 4, (j % 4) * P:(j % 4 + 1) * P], RV[:, c, j * P:(j + 1) * P], IDENT)
                last.then_inc(ot_done, 1)

            inner(0)
            for c in range(4):
                chunk(c)
                if c < 3:
                    inner(c + 1)
                if c:
                    turn(c - 1)
            turn(3)
            pe.wait_ge(in_masked, lay * 5 + 4)
            pe.wait_ge(o_scaled, lay * 5 + 4)
            for h in range(R_HEADS):
                last = pe.matmul(PS[0:NS, 4, h * NS:(h + 1) * NS], RTT[:, 4 + h, SEQ:N], RTT[:, h, SEQ:N],
                                 start=True, stop=True)
            last.then_inc(in_done, 1)
            hold(pe, in_masked, lay * 5 + 5)
            for h in range(R_HEADS):
                pe.matmul(PS[32 * h:32 * h + 32, 5, 0:256], IND[0:NS, h * NS:(h + 1) * NS],
                          RV[0:NS, TT - 1, h * 256:(h + 1) * 256], start=True, stop=False)
            pe.wait_ge(qm_ready, lay + 1)
            pe.wait_ge(ot_act, lay * 5 + 4)
            pe.wait_ge(ot_dve, lay * 5 + 4)
            for b in range(DEC_B):
                pe.wait_ge(s0_in[b % 4], (lay * 2 + b // 4 + 1) * 16)
                for h in range(R_HEADS):
                    last = pe.matmul(PS[32 * h:32 * h + 32, 5, 0:256], QM[:, h, b * 32:(b + 1) * 32],
                                     S0[:, b % 4, h, :], start=False, stop=b == DEC_B - 1)
                if b == DEC_B - 1:
                    last.then_inc(so_done, 1)
                pe.wait_ge(km_ready, lay * 8 + b + 1)
                if b:
                    pe.wait_ge(sn_ready, lay * 8 + b)
                for h in range(R_HEADS):
                    last = pe.matmul(PS[:, 2 + h // 2, (h % 2) * 256:(h % 2 + 1) * 256],
                                     KM[0:NS, b % 2, h * P:(h + 1) * P], RV[0:NS, TT - 1, h * 256:(h + 1) * 256],
                                     start=True, stop=True)
                last.then_inc(ss_done, 1)
                if b % 2 == 0:
                    split_ready(U0["rg"] + b // 2)
                feature_tile(T0["rg"] + b, 3 * (b % 2), b // 2 % 2, UC, (b % 2) * P, kk, x, depth=2)
            pe.wait_ge(o_scaled, lay * 5 + 5)
            for j in range(2):
                last = pe.transpose(PS[:, 4 + j, 0:P], QM[:, 0, j * P:(j + 1) * P], IDENT)
            last.then_inc(ot_done, 1)
            hold(pe, sn_ready, lay * 8 + 8)
            hold(pe, tile_free, lay * NT + T0["br_ret"] + 2)
            hold(pe, ot_act, lay * 5 + 5)
            hold(pe, ot_dve, lay * 5 + 5)
            for name, rhs, ks in (("br_ret", (ROH, ROL), kk), ("br_att", (MOH, MOL), kk[:4])):
                with pe.Fori(0, 4) as i:
                    unit2(U0[name] + 2 * i, 0, T0[name] + 4 * i, kk, x)
                    pe.wait_ge(x_lo, lay * NX + (X0["rg"] + KT))
                    unit2(U0[name] + 2 * i + 1, 1, T0[name] + 4 * i + 2, ks, rhs)
            for j in range(2):
                if j == 0:
                    unit2_late(U0["out"], 0, T0["out"], (ROH, ROL), lay * NX + X0["br_att"] + KT)
                else:
                    unit2(U0["out"] + j, j, T0["out"] + 2 * j, kk, (ROH, ROL))
            with pe.Fori(1, 2) as i:
                for j in range(2):
                    unit2(U0["out"] + 2 * i + j, j, T0["out"] + 4 * i + 2 * j, kk, (ROH, ROL))
            unit2_late(U0["gu"], 0, T0["gu"], x, lay * NX + X0["out"] + KT)
            square_sums(2 * lay + 2)
            spread(2 * lay + 2, (5, 6))
            pe.wait_ge(rt_taken, 2 * lay + 2)
            unit2(U0["gu"] + 1, 1, T0["gu"] + 2, kk, x)
            with pe.Fori(1, FT // 2) as i:
                for j in range(2):
                    unit2(U0["gu"] + 2 * i + j, j, T0["gu"] + 4 * i + 2 * j, kk, x)
            with pe.Fori(0, KT // 2) as i:
                for m in range(2):
                    for j in range(2):
                        u, tile = U0["down"] + 4 * i + 2 * m + j, T0["down"] + 2 * i + m
                        split_ready(u)
                        pe.wait_ge(x_lo, lay * NX + (X0["gu"] + (FT // 2 if j == 0 else FT)))
                        last = feature_tile(tile, m, j, P, 0, range(11 * j, 11 * j + 11), (AH, AL), j == 0, j == 1,
                                            depth=2)
                        if j == 0:
                            last.then_inc(half_done, 1)
        square_sums(2 * DEPTH + 1)

        for t, n in enumerate(ROWS):
            pe.wait_ge(xg_ready, 1)
            if t >= 2:
                pe.wait_ge(o_scaled, DEPTH * 5 + t - 1)
            for m in range(KT):
                last = pe.transpose(PS[0:n, 2 * (t % 2) + m // 4, (m % 4) * P:(m % 4 + 1) * P],
                                    XT[:, m, t * P:t * P + n], IDENT)
            last.then_inc(tr_done, 1)

    @block.scalar
    def _(act):
        def x_parts(m, gcol, ready, squared):
            hold(act, *ready)
            act.activation(XH[:, m, :], XT[:, m, :], ACT.Copy, scale=GT[:, gcol])
            hold(act, sq_added, squared)
            act.activation(EB[:, 0, :], XT[:, m, :], ACT.Square).then_inc(hi_val, 1)

        act.wait_ge(g_ready, 1)
        for m in range(KT):
            x_parts(m, slice(m, m + 1), (xt_copied, m + 1), m)
        act.wait_ge(landed[0], 32)
        act.activation(WH[:, 0, :], RAW[:, 0, :], ACT.Copy).then_inc(hi_ready, 1)

        with act.Fori(0, DEPTH) as lay:
            def split(u, slot, n, prev):
                act.wait_ge(landed[slot], (lay * NU // 2 + u // 2 + 1) * 32 if isinstance(u, int)
                            else lay * (NU * 16) + u * 16 + (32 - 16 * slot))
                act.wait_ge(*prev)
                act.activation(WH[:, slot, 0:n], RAW[:, slot, 0:n], ACT.Copy).then_inc(hi_ready, 1)

            def ahead(name, i, j, per, n=8 * UC):
                split(2 * i + (U0[name] + j + 1), (j + 1) % 2, n,
                      (tile_done, lay * NT + T0[name] + per * j + i * (2 * per)))

            def done(tile):
                act.wait_ge(tile_done, lay * NT + tile + 1)

            def rotated_tiles(name, i, j, scale, r0, banks=(0, 2)):
                for t, n in enumerate(ROWS):
                    tile = i * (2 * TT) + (T0[name] + j * TT + t)
                    bank = (j * TT + t) % 2
                    done(tile)
                    act.wait_ge(rot_free, lay * 40 + i * (2 * TT) + (r0 + j * TT + t + 1))
                    act.activation(XS[0:n, bank, :], PS[0:n, banks[bank], 0:UC], ACT.Copy,
                                   scale=scale[0:n, t:t + 1]).then_inc(tile_free, 1)

            def value_tiles(name, i, j, dst):
                for t, n in enumerate(ROWS):
                    hold(act, tile_done, lay * NT + i * (2 * TT) + (T0[name] + j * TT + t + 1))
                    act.activation(dst[0:n, t, bass.ds(i * (2 * UC) + j * UC, UC)], PS[0:n, 2 * ((j * TT + t) % 2), 0:UC],
                                   ACT.Copy, scale=RT[0:n, t:t + 1]).then_inc(tile_free, 1)

            def copy_transposes(dst, base):
                for j in range(0, 8, 2):
                    act.wait_ge(tr_done, lay * 16 + base + j + 1)
                    act.activation(dst[:, j, 0:SEQ], PS[:, 4, :], ACT.Copy)
                    act.activation(dst[:, j, SEQ:N], PS[:, 5, 0:NS], ACT.Copy).then_inc(tr_act, 1)

            with act.Fori(0, 2) as i:
                for j in range(2):
                    ahead("mqk", i, j, TT)
                    act.wait_ge(rt_ready, lay + 1)
                    rotated_tiles("mqk", i, j, RT, 0)
            for j in range(2):
                ahead("mv", 0, j, TT)
                value_tiles("mv", 0, j, MV)
            copy_transposes(MT, 0)

            def exp(n):
                w = (n % 4 + 1) * P
                act.wait_ge(s_max, lay * 32 + n + 1)
                if n >= 4:
                    act.wait_ge(pt_done, lay * 32 + n - 3)
                act.activation(PR[:, n % 4, 0:w], PS[:, 2 + n % 4, 0:w], ACT.Exp, bias=NM[:, n % 4:n % 4 + 1],
                               scale=M_SCALE, accum_out=RSUM[:, n % 4:n % 4 + 1]).then_inc(s_exp, 1)

            act.wait_ge(kv_out, lay * 64 + 64)

            def attended(hp):
                act.wait_ge(pv_done, lay * 4 + hp + 1)
                act.activation(MOH[:, hp, 0:SEQ], PS[:, 1 + 6 * (hp % 2), :], ACT.Copy).then_inc(mo_hi, 1)

            exp(0)
            for n in range(32):
                h, t = divmod(n, 4)
                if n + 1 < 32:
                    exp(n + 1)
                act.wait_ge(pt_done, lay * 32 + n + 1)
                act.activation(PT[:, h % 2, 0:t + 1, t * P:(t + 1) * P],
                               PS[:, 6 * (1 - n % 2), 0:(t + 1) * P].rearrange("p (k c) -> p k c", c=P),
                               ACT.Copy).then_inc(pt_evac, 1)
                if t == 3 and h and h % 2 == 0:
                    attended(h // 2 - 1)
            attended(3)

            def exp_group(g):
                act.wait_ge(sel_ready, lay * 2 + g + 1)
                for k in range(4):
                    act.activation(SP_[:, g, k * 256:(k + 1) * 256],
                                   PS[:, 4 + 2 * g + k // 2, (k % 2) * 256:(k % 2 + 1) * 256],
                                   ACT.Exp, bias=BIAS[:, k:k + 1], scale=M_SCALE, accum_out=ES[:, k:k + 1])
                act.activation(SP_[:, g, PAST:PAST + NS], PS[:, 3, g * NS:(g + 1) * NS], ACT.Exp, bias=BIAS[:, 4:5],
                               scale=M_SCALE, accum_out=ES[:, 4:5]).then_inc(e_done, 1)

            def attended_sample(g):
                act.wait_ge(mos_done, lay * 2 + g + 1)
                act.activation(MOH[:, :, SEQ + 16 * g:SEQ + 16 * (g + 1)],
                               PS[:, 3, 64 + g * 64:128 + g * 64].rearrange("p (k c) -> p k c", c=16),
                               ACT.Copy).then_inc(mos_hi, 1)

            for q in range(NG * N_PAGES):
                for b in (0, 2):
                    act.wait_ge(kt_done, lay * 64 + 4 * q + b + 1)
                    if q >= 2:
                        act.wait_ge(sc_done, lay * 18 + q - 1 + (q >= 10))
                    act.activation(KTT[q % 2][:, b, :, :], PS[:, (4 * q + b) % 3, :].rearrange("p (k c) -> p k c", c=P),
                                   ACT.Copy).then_inc(kt_act, 1)
                if q == N_PAGES + 3:
                    exp_group(0)
            for g in range(NG):
                act.wait_ge(pts_done, lay * 4 + 2 * g + 1)
                act.activation(PTS[:, 0:4, :], PS[:, 0, :].rearrange("p (k c) -> p k c", c=P), ACT.Copy)\
                    .then_inc(pts_act, 1)
                if g == 0:
                    exp_group(1)
                ahead("rqk", 0, g, TT)
                if g:
                    attended_sample(0)
                rotated_tiles("rqk", 0, g, RT, 20, (5, 7))
            attended_sample(1)

            for j in range(2):
                ahead("rqk", 1, j, TT)
                rotated_tiles("rqk", 1, j, RTK, 20)
            with act.Fori(0, 2) as i:
                for j in range(2):
                    ahead("rv", i, j, TT)
                    value_tiles("rv", i, j, RV)
            copy_transposes(RTT, 8)

            def scale_out(c, src, dst, k):
                act.wait_ge(o_done if c < 4 else so_done, lay * 4 + c + 1 if c < 4 else lay + 1)
                for h in range(k):
                    last = act.activation(EB[:].rearrange("p a n -> p (a n)")[:, h * 256:(h + 1) * 256], src(h), ACT.Square, accum_out=SSQ[:, h:h + 1])
                last.then_inc(ssq_ready, 1)
                act.wait_ge(rms_ready, lay * 5 + c + 1)
                if c < 4:
                    act.wait_ge(st_done, lay * 4 + c + 1)
                for h in range(k):
                    last = act.activation(dst(h), src(h), ACT.Copy, scale=RRS[:, h:h + 1])
                last.then_inc(o_scaled, 1)

            def out_turned(c):
                act.wait_ge(ot_done, lay * 5 + c + 1)
                act.activation(ROT[:, 0:4, c * P:(c + 1) * P], PS[:, 0, :].rearrange("p (k c) -> p k c", c=P),
                               ACT.Copy).then_inc(ot_act, 1)

            for c in range(4):
                scale_out(c, lambda h: PS[:, 5 + h // 2, (h % 2) * 256:(h % 2 + 1) * 256],
                          lambda h: RV[:, c, h * 256:(h + 1) * 256], R_HEADS)
                if c:
                    out_turned(c - 1)
            out_turned(3)

            def sig(tile, dst, src, e):
                act.wait_ge(tile_free, lay * NT + tile + 3)
                act.activation(EB[:, dst, :], EA[:, src, :], ACT.Sigmoid).then_inc(sig_done, 1)

            def gate_tile(k):
                sig(k + T0["rg"], k % 2, k % 2, k)
                act.wait_ge(val_ready, lay * NVAL + k + (V0N["rg"] + 1))
                act.activation(ROH[:, k, 0:SEQ], ROT[:, k, 0:SEQ], ACT.Copy).then_inc(hi_val, 1)

            for b in range(DEC_B):
                if b:
                    gate_tile(b - 1)
                if b % 2 == 0:
                    ahead("rg", b // 4, b // 2 % 2, 2)
            act.wait_ge(so_done, lay + 1)
            act.activation(QM[:, 1, :], PS[:, 5, 0:256], ACT.Square, accum_out=SSQ[:, 0:1]).then_inc(ssq_ready, 1)
            act.wait_ge(rms_ready, lay * 5 + 5)
            act.activation(QM[:, 0, :], PS[:, 5, 0:256], ACT.Copy, scale=RRS[:, 0:1]).then_inc(o_scaled, 1)
            gate_tile(7)
            act.wait_ge(ot_done, lay * 5 + 5)
            act.activation(ROT[:, 0:8:2, SEQ:N], PS[:, 4, 0:P].rearrange("p (h c) -> p h c", c=NS),
                           ACT.Copy).then_inc(ot_act, 1)
            act.wait_ge(rot_gated, lay + 1)
            act.activation(ROH[:, :, SEQ:N], ROT[:, :, SEQ:N], ACT.Copy).then_inc(hi_rot, 1)

            act.wait_ge(st_out, lay * 16 + 16)
            with act.Fori(0, 4) as i:
                for j in range(2):
                    ahead("br_ret", i, j, 2)
                    if j == 0:
                        for m in range(2):
                            sig(4 * i + (T0["br_ret"] + m), m, m, 0)
            with act.Fori(0, 4) as i:
                for j in range(2):
                    ahead("br_att", i, j, 2, 4 * UC if j == 0 else 8 * UC)
                    for m in range(2):
                        if j == 0:
                            sig(4 * i + (T0["br_att"] + m), m, m, 0)
                        else:
                            hold(act, val_ready, lay * NVAL + 2 * i + (V0N["br_att"] + m + 1))
                            act.activation(ROH[:, bass.ds(2 * i + m, 1), :], G1[:, bass.ds(2 * i + m, 1), :],
                                           ACT.Copy).then_inc(hi_val, 1)
            with act.Fori(0, 2) as i:
                for j in range(2):
                    ahead("out", i, j, 2)
                    for m in range(2):
                        k = 4 * i + (2 * j + m)
                        x_parts(bass.ds(k, 1), bass.ds(8 * lay + k + 16, 1),
                                (tile_free, lay * NT + k + (T0["out"] + 3)), (2 * lay + 1) * KT + k)
            with act.Fori(0, FT // 2) as i:
                for j in range(2):
                    ahead("gu", i, j, 2)
                    sig(4 * i + (2 * j + T0["gu"]), 0, 0, 0)
                    hold(act, val_ready, lay * NVAL + 2 * i + (V0N["gu"] + j + 1))
                    act.activation(AH[:, bass.ds(2 * i + j, 1), :], EA[:, 1:2, :], ACT.Copy).then_inc(hi_val, 1)

            def down(i, m):
                k = 2 * i + m
                split(4 * i + (U0["down"] + 2 * m + 1), 1, 11 * P, (tile_done, lay * NT + k + T0["down"]))
                split(4 * i + (U0["down"] + 2 * m + 2), 0, 8 * UC, (half_done, lay * KT + k + 1))
                x_parts(bass.ds(k, 1), bass.ds(24 * lay + k + 8, 1),
                        (tile_free, lay * NT + k + (T0["down"] + 3)), (2 * lay + 2) * KT + k)

            with act.Fori(0, KT // 2) as i:
                for m in range(2):
                    down(i, m)

        for t, n in enumerate(ROWS):
            act.wait_ge(tr_done, DEPTH * 16 + t + 1)
            if t == 0:
                act.wait_ge(nrt, 2 * DEPTH + 1)
            if t >= 2:
                act.wait_ge(y_out, 16 * (t - 1))
            act.activation(YO[0:n, t % 2, :].rearrange("p (a c) -> p a c", a=2),
                           PS[0:n, 2 * (t % 2):2 * (t % 2) + 2, :], ACT.Copy,
                           scale=RT[0:n, t:t + 1]).then_inc(o_scaled, 1)

    @block.vector
    def _(dve):
        own = Order(dve, dve_own)
        pair = [PS[:, 2 * p:2 * p + 2, 0:HALF] for p in range(4)]

        def halves(a):
            return a.rearrange("p (h c) -> p h c", h=2)

        RB = halves(RSTDB[:])

        def variance(count):
            dve.wait_ge(nsum, count)
            dve.tensor_scalar(VAR[:, 0:TT - 1], PS[:, 4, 0:TT - 1], 1.0 / D_MODEL, EPS, ALU.mult, ALU.add)
            dve.tensor_scalar(VAR[0:NS, TT - 1:TT], PS[0:NS, 4, TT - 1:TT], 1.0 / D_MODEL, EPS,
                              ALU.mult, ALU.add).then_inc(nvar, 1)

        def spread_rt(count):
            dve.wait_ge(nrt, count)
            dve.tensor_tensor(DIAG, IDENT.unsqueeze(1).to_broadcast([P, TT, P]),
                              RT.unsqueeze(2).to_broadcast([P, TT, P]), ALU.mult).then_inc(ndiag, 1)

        def take_rt(count, banks):
            dve.wait_ge(nbc, count)
            dve.tensor_copy(RSTDB[:, 0:SEQ], PS[:, banks[0], :])
            dve.tensor_copy(RSTDB[:, SEQ:N], PS[:, banks[1], 0:NS]).then_inc(rt_taken, 1)

        def low_x(m, gcol, hi, squared):
            dve.wait_ge(hi_val, hi)
            dve.scalar_tensor_tensor(out=XL[:, m, :], in0=XT[:, m, :], scalar=GT[:, gcol],
                                     in1=XH[:, m, :].bitcast(F32), op0=ALU.mult, op1=ALU.subtract).then_inc(x_lo, 1)
            dve.wait_ge(sq_added, squared)
            dve.tensor_tensor(EB[:, 1, :], EB[:, 1, :], EB[:, 0, :], ALU.add).then_inc(sq_added, 1)

        dve.memset(SM[:, 90:91], 0.0).then_inc(lo_ready, 2)
        own.mark(dve.memset(VAR, 1.0))
        own.mark(dve.memset(EB[:, 1, :], 0.0))
        dve.wait_ge(xt_done, 1)
        dve.tensor_copy(GT[:], PS[:, 0, 0:40]).then_inc(g_ready, 1)
        dve.wait_ge(g_ready, 1)
        own.wait()

        def input_tile(m):
            dve.wait_ge(xt_done, m + 2)
            dve.tensor_copy(XT[:, m, 0:SEQ], PS[:, 4 + 2 * (m % 2), :])
            dve.tensor_copy(XT[:, m, SEQ:N], PS[:, 5 + 2 * (m % 2), 0:NS]).then_inc(xt_copied, 1)

        input_tile(0)
        for m in range(KT):
            if m + 1 < KT:
                input_tile(m + 1)
            low_x(m, slice(m, m + 1), m + 1, m)

        dve.wait_ge(hi_ready, 1)
        dve.tensor_tensor(WL[:, 0, :], RAW[:, 0, :], WH[:, 0, :].bitcast(F32), ALU.subtract).then_inc(lo_ready, 1)

        with dve.Fori(0, DEPTH) as lay:
            own.base, own.n, start = lay * LAYER_MARKS + own.n, 0, own.n

            def split(u, slot, n):
                dve.wait_ge(hi_ready, lay * NU + u + 1)
                dve.tensor_tensor(WL[:, slot, 0:n], RAW[:, slot, 0:n], WH[:, slot, 0:n].bitcast(F32),
                                  ALU.subtract).then_inc(lo_ready, 1)

            def ahead(name, i, j, n=8 * UC):
                split(2 * i + (U0[name] + j + 1), (j + 1) % 2, n)

            def rotate(src, dst, cos, sin, n, heads, pairs, before):
                s, d = pairs(src), pairs(dst)
                w = s[0].shape[-1]
                c = cos.unsqueeze(1).to_broadcast([n, heads, w])
                z = sin.unsqueeze(1).to_broadcast([n, heads, w])
                a1, a2 = (RO1[0:n, k * 128:(k + 1) * 128].rearrange("p (h w) -> p h w", h=heads) for k in range(2))
                b1, b2 = (RO2[0:n, k * 128:(k + 1) * 128].rearrange("p (h w) -> p h w", h=heads) for k in range(2))
                dve.wait_ge(rot_free, before)
                dve.tensor_tensor(a1, s[0], c, ALU.mult)
                dve.tensor_tensor(a2, s[1], z, ALU.mult)
                dve.tensor_tensor(b1, s[1], c, ALU.mult)
                own.mark(dve.tensor_tensor(b2, s[0], z, ALU.mult))
                own.wait()
                dve.tensor_tensor(d[0], a1, a2, ALU.subtract)
                dve.tensor_tensor(d[1], b1, b2, ALU.add).then_inc(rot_free, 1)

            def rope_pairs(a):
                v = a.rearrange("p (h z w) -> p h z w", z=2, w=32)
                return v[:, :, 0, :], v[:, :, 1, :]

            def retnet_pairs(a):
                v = a.rearrange("p (h w z) -> p h w z", z=2, w=64)
                return v[:, :, :, 0], v[:, :, :, 1]

            def rotated_tiles(name, i, j, dst, col, tables, heads, pairs, r0):
                for t, n in enumerate(ROWS):
                    tile = i * (2 * TT) + (T0[name] + j * TT + t)
                    dve.wait_ge(tile_free, lay * NT + tile + 3)
                    w = tables[0].shape[-1] // TT
                    rotate(XS[0:n, (j * TT + t) % 2, :], dst[0:n, t, bass.ds(col, UC)],
                           tables[0][0:n, t * w:(t + 1) * w], tables[1][0:n, t * w:(t + 1) * w], n, heads, pairs,
                           lay * 40 + i * (2 * TT) + (r0 + j * TT + t + 2))

            def copy_transposes(dst, base):
                for j in range(1, 8, 2):
                    dve.wait_ge(tr_done, lay * 16 + base + j + 1)
                    dve.tensor_copy(dst[:, j, 0:SEQ], PS[:, 6, :])
                    dve.tensor_copy(dst[:, j, SEQ:N], PS[:, 7, 0:NS]).then_inc(tr_dve, 1)

            variance(2 * lay + 1)
            dve.wait_ge(nrt, 2 * lay + 1)
            dve.tensor_scalar(RTK, RT, R_DK ** -0.5, None, ALU.mult).then_inc(rt_ready, 1)
            with own.loop(2, 2 * TT) as i:
                for j in range(2):
                    ahead("mqk", i, j)
                    dve.wait_ge(cl_in, lay * 16 + 16)
                    rotated_tiles("mqk", i, j, QK, i * (2 * UC) + j * UC, (cl("cosm"), cl("sinm")), 4, rope_pairs, 0)
            for j in range(2):
                ahead("mv", 0, j)
            copy_transposes(MT, 0)
            spread_rt(2 * lay + 1)
            take_rt(2 * lay + 1, (1, 7))

            def row_max(n):
                t, b = n % 4, n % 4
                dve.wait_ge(s_done, lay * 32 + n + 1)
                d = PS[:, 2 + b, t * P:(t + 1) * P]
                own.mark(dve.tensor_tensor(d, d, cl("causal"), ALU.add))
                own.wait()
                own.mark(dve.tensor_reduce(MX[:, b:b + 1], PS[:, 2 + b, 0:(t + 1) * P], AX, ALU.max))
                own.wait()
                dve.tensor_scalar(NM[:, b:b + 1], MX[:, b:b + 1], -M_SCALE, None, ALU.mult).then_inc(s_max, 1)

            def attended(hp):
                dve.wait_ge(mo_hi, lay * 4 + hp + 1)
                dve.tensor_tensor(MOL[:, hp, 0:SEQ], PS[:, 1 + 6 * (hp % 2), :], MOH[:, hp, 0:SEQ].bitcast(F32),
                                  ALU.subtract).then_inc(mo_lo, 1)

            row_max(0)
            row_max(1)
            for n in range(32):
                h, t, b = n // 4, n % 4, n % 4
                if n + 2 < 32:
                    row_max(n + 2)
                dve.wait_ge(s_exp, lay * 32 + n + 1)
                own.mark(dve.reciprocal(RINV[:, b:b + 1], RSUM[:, b:b + 1]))
                own.wait()
                p = PR[:, b, 0:(t + 1) * P]
                dve.tensor_scalar(p, p, RINV[:, b:b + 1], None, ALU.mult).then_inc(s_prob, 1)
                if t == 0 and h > 1 and h % 2:
                    attended(h // 2 - 1)
            attended(3)

            dve.wait_ge(kv_out, lay * 64 + 64)
            dve.wait_ge(tr_act, lay * 8 + 4)
            dve.wait_ge(mo_lo, lay * 4 + 4)
            own.mark(dve.memset(QB[:], 0.0))
            own.wait()
            for hp in range(4):
                for z in range(2):
                    r = slice(64 * z, 64 * z + 64)
                    last = dve.tensor_copy(
                        QB[r, hp, :].rearrange("p (b c) -> p b c", c=32)[:, :, 8 * hp + 4 * z:8 * hp + 4 * z + 4],
                        MT[r, hp, SEQ:N].rearrange("p (b q) -> p b q", q=DEC_L))
            last.then_inc(qb_ready, 1)

            def select(g, part):
                blocks = PS[:, 4 + 2 * g:6 + 2 * g, :].rearrange("p a (k c) -> p (a k) c", c=M_BLOCK)
                mine = PS[:, 3, g * NS:(g + 1) * NS]
                if part == 0:
                    dve.wait_ge(sc_done, lay * 18 + 9 * g + 9)
                    own.mark(dve.tensor_tensor(mine, mine, cl("own")[:, g * NS:(g + 1) * NS], ALU.add))
                    own.mark(dve.tensor_reduce(BS, blocks, AX, ALU.add))
                elif part == 1:
                    own.mark(dve.tensor_reduce(BM[:, 0:4], blocks, AX, ALU.max))
                    own.wait()
                    own.mark(dve.tensor_reduce(BM[:, 4:5], mine, AX, ALU.max))
                    own.mark(dve.tensor_reduce(T1A[:, 0:1], BS, AX, ALU.min))
                else:
                    own.wait()
                    own.mark(dve.scalar_tensor_tensor(out=EQ, in0=BS, scalar=T1A[:, 0:1], in1=cl("rank"),
                                                      op0=ALU.is_equal, op1=ALU.mult))
                    own.wait()
                    own.mark(dve.tensor_reduce(T1A[:, 1:2], EQ, AX, ALU.max))
                    own.wait()
                    own.mark(dve.tensor_scalar(PEN, EQ, T1A[:, 1:2], -BIG, ALU.is_equal, ALU.mult))
                    own.wait()
                    own.mark(dve.tensor_tensor(BM[:, 0:4], BM[:, 0:4], PEN, ALU.add))
                    own.wait()
                    own.mark(dve.tensor_reduce(T1A[:, 0:1], BM, AX, ALU.max))
                    own.wait()
                    own.mark(dve.tensor_scalar(BIAS[:, 4:5], T1A[:, 0:1], -M_SCALE, None, ALU.mult))
                    own.wait()
                    dve.tensor_scalar(BIAS[:, 0:4], PEN, BIAS[:, 4:5], None, ALU.add).then_inc(sel_ready, 1)

            def inverse_sum(g):
                dve.wait_ge(e_done, lay * 2 + g + 1)
                own.mark(dve.tensor_reduce(SRI[:, g:g + 1], ES, AX, ALU.add))
                own.wait()
                own.mark(dve.reciprocal(SRI[:, g:g + 1], SRI[:, g:g + 1]))

            def own_head(g):
                own.wait()
                dve.wait_ge(pts_done, lay * 4 + 2 * g + 2)
                dve.scalar_tensor_tensor(out=OS[:].rearrange("p (h c) -> p h c", c=M_DH),
                                         in0=PS[:, 4 + 2 * g, :].rearrange("p (h c) -> p h c", c=M_DH),
                                         scalar=SRI[:, g:g + 1],
                                         in1=cl("headm").unsqueeze(2).to_broadcast([P, 8, M_DH]),
                                         op0=ALU.mult, op1=ALU.mult).then_inc(os_ready, 1)

            def attended_sample(g):
                dve.wait_ge(mos_hi, lay * 2 + g + 1)
                cols = slice(SEQ + 16 * g, SEQ + 16 * (g + 1))
                dve.tensor_tensor(MOL[:, :, cols],
                                  PS[:, 3, 64 + g * 64:128 + g * 64].rearrange("p (k c) -> p k c", c=16),
                                  MOH[:, :, cols].bitcast(F32), ALU.subtract).then_inc(mos_lo, 1)

            for q in range(NG * N_PAGES):
                for b in (1, 3):
                    dve.wait_ge(kt_done, lay * 64 + 4 * q + b + 1)
                    if q >= 2:
                        dve.wait_ge(sc_done, lay * 18 + q - 1 + (q >= 10))
                    dve.tensor_copy(KTT[q % 2][:, b, :, :], PS[:, (4 * q + b) % 3, :].rearrange("p (k c) -> p k c", c=P))\
                        .then_inc(kt_dve, 1)
                if N_PAGES < q <= N_PAGES + 3:
                    select(0, q - N_PAGES - 1)
            for g in range(NG):
                dve.wait_ge(pts_done, lay * 4 + 2 * g + 1)
                dve.tensor_copy(PTS[:, 4:8, :], PS[:, 1, :].rearrange("p (k c) -> p k c", c=P))
                dve.tensor_copy(PTS[0:NS, 8, :], PS[0:NS, 2, 0:P]).then_inc(pts_dve, 1)
                if g == 0:
                    inverse_sum(0)
                    for part in range(3):
                        select(1, part)
                    inverse_sum(1)
                    ahead("rqk", 0, 0)
                else:
                    own_head(0)
                    ahead("rqk", 0, 1)
                    attended_sample(0)
                rotated_tiles("rqk", 0, g, RQ, g * UC, (cl("cosr"), cl("sinr")), 2, retnet_pairs, 20)
            own_head(1)
            attended_sample(1)

            for j in range(2):
                ahead("rqk", 1, j)
                rotated_tiles("rqk", 1, j, RK, j * UC, (cl("cosr"), cl("sinr")), 2, retnet_pairs, 20)
            with own.loop(2, 0) as i:
                for j in range(2):
                    ahead("rv", i, j)
            copy_transposes(RTT, 8)
            dve.wait_ge(tr_done, lay * 16 + 16)
            for t, n in enumerate(ROWS):
                k = RK[0:n, t, :].rearrange("p (h c) -> p h c", c=P)
                dec = (cl("kdec") if t < TT - 1 else cl("kdecs"))[0:n].unsqueeze(2).to_broadcast([n, 4, P])
                dve.tensor_tensor(k, k, dec, ALU.mult).then_inc(kd_ready, 1)
            dve.wait_ge(tr_act, lay * 8 + 8)
            dve.wait_ge(tr_dve, lay * 8 + 8)

            def masked(c):
                dve.wait_ge(in_done, lay * 5 + c + 1)
                if c:
                    dve.wait_ge(o_done, lay * 4 + c)
                    dve.tensor_tensor(QD.rearrange("p (h c) -> p h c", c=P), RTT[:, 0:4, c * P:(c + 1) * P],
                                      cl("qdt").rearrange("p (h c) -> p h c", c=P), ALU.mult)
                dve.tensor_tensor(IND, PS[:, 4, :], cl("dect"), ALU.mult).then_inc(in_masked, 1)

            def variances(c, k):
                dve.wait_ge(ssq_ready, lay * 5 + c + 1)
                dve.tensor_scalar(RMS[:, 0:k], SSQ[:, 0:k], 1.0 / R_DV, EPS, ALU.mult, ALU.add).then_inc(var_ready, 1)

            def out_turned(c):
                dve.wait_ge(ot_done, lay * 5 + c + 1)
                dve.tensor_copy(ROT[:, 4:8, c * P:(c + 1) * P], PS[:, 1, :].rearrange("p (k c) -> p k c", c=P))\
                    .then_inc(ot_dve, 1)

            masked(0)
            for c in range(4):
                variances(c, R_HEADS)
                dve.wait_ge(st_done, lay * 4 + c + 1)
                if c == 0:
                    dve.tensor_copy(ST[:].rearrange("p (a b) c -> p a (b c)", a=2), PS[:, 2:4, :]).then_inc(st_ready, 1)
                else:
                    dve.wait_ge(st_ready, lay * 4 + c)
                    for h in range(R_HEADS):
                        last = dve.scalar_tensor_tensor(
                            out=ST[:, h, :], in0=ST[:, h, :], scalar=G_CHUNK[h],
                            in1=PS[:, 2 + h // 2, (h % 2) * 256:(h % 2 + 1) * 256], op0=ALU.mult, op1=ALU.add)
                    last.then_inc(st_ready, 1)
                if c < 3:
                    masked(c + 1)
                if c:
                    out_turned(c - 1)
            out_turned(3)
            own.mark(dve.memset(QM[:], 0.0))
            own.wait()
            dve.tensor_tensor(diag(QM, 0), RTT[:, 0:4, SEQ:N].rearrange("p h (b q) -> p h b q", q=DEC_L),
                              cl("qds").rearrange("p (h b q) -> p h b q", h=4, q=DEC_L), ALU.mult).then_inc(qm_ready, 1)
            dve.wait_ge(in_done, lay * 5 + 5)
            dve.tensor_tensor(IND[0:NS, 0:P], PS[0:NS, 4, 0:P], cl("decs", NS), ALU.mult).then_inc(in_masked, 1)

            def key_of(b):
                if b >= 2:
                    dve.wait_ge(ss_done, lay * 8 + b - 1)
                dve.tensor_scalar(KM[0:NS, b % 2, :], RK[0:NS, TT - 1, :], cl("seqm", NS)[:, b:b + 1], None,
                                  ALU.mult).then_inc(km_ready, 1)

            dve.wait_ge(kd_ready, lay * 5 + 5)
            def gate_tile(k):
                m = k % 2
                done(k + T0["rg"])
                dve.tensor_tensor(halves(EA[:, m, :]), pair[3 * m], RB, ALU.mult).then_inc(tile_free, 1)
                dve.wait_ge(sig_done, lay * NSIG + k + (S0N["rg"] + 1))
                own.mark(dve.tensor_tensor(EA[:, m, :], EA[:, m, :], EB[:, m, :], ALU.mult))
                own.wait()
                own.mark(dve.tensor_copy(SGATE[:, k, :], EA[:, m, SEQ:N]))
                dve.tensor_tensor(ROT[:, k, 0:SEQ], EA[:, m, 0:SEQ], ROT[:, k, 0:SEQ], ALU.mult).then_inc(val_ready, 1)

            def done(tile):
                dve.wait_ge(tile_done, lay * NT + tile + 1)

            key_of(0)
            for b in range(DEC_B):
                if b + 1 < DEC_B:
                    key_of(b + 1)
                dve.wait_ge(ss_done, lay * 8 + b + 1)
                for h in range(R_HEADS):
                    last = dve.scalar_tensor_tensor(
                        out=S0[:, b % 4, h, :], in0=S0[:, b % 4, h, :], scalar=G_STEP[h],
                        in1=PS[:, 2 + h // 2, (h % 2) * 256:(h % 2 + 1) * 256], op0=ALU.mult, op1=ALU.add)
                last.then_inc(sn_ready, 1)
                if b:
                    gate_tile(b - 1)
                if b % 2 == 0:
                    ahead("rg", b // 4, b // 2 % 2)
            variances(4, 1)
            gate_tile(7)
            dve.wait_ge(ot_done, lay * 5 + 5)
            dve.tensor_copy(ROT[:, 1:8:2, SEQ:N], PS[:, 5, 0:P].rearrange("p (h c) -> p h c", c=NS)).then_inc(ot_dve, 1)
            dve.wait_ge(ot_act, lay * 5 + 5)
            dve.wait_ge(ot_dve, lay * 5 + 5)
            own.wait()
            dve.tensor_tensor(ROT[:, :, SEQ:N], ROT[:, :, SEQ:N], SGATE[:], ALU.mult).then_inc(rot_gated, 1)

            def scaled(tile, p, dst):
                done(tile)
                dve.tensor_tensor(halves(dst), pair[p], RB, ALU.mult).then_inc(tile_free, 1)

            dve.wait_ge(st_out, lay * 16 + 16)
            dve.wait_ge(hi_val, lay * NX + X0["rg"] + KT)
            dve.wait_ge(hi_rot, lay + 1)
            for b in range(4):
                dve.wait_ge(sn_out[b], lay * 32 + 32)
            for k in range(KT):
                dve.tensor_tensor(ROL[:, k, :], ROT[:, k, :], ROH[:, k, :].bitcast(F32), ALU.subtract)\
                    .then_inc(x_lo, 1)
            hold(dve, x_lo, lay * NX + X0["rg"] + KT)
            with own.loop(4, 0) as i:
                for j in range(2):
                    ahead("br_ret", i, j)
                    for m in range(2):
                        tile = 4 * i + (T0["br_ret"] + 2 * j + m)
                        if j == 0:
                            scaled(tile, m, EA[:, m, :])
                        else:
                            dve.wait_ge(sig_done, lay * NSIG + 2 * i + (S0N["br_ret"] + m + 1))
                            done(tile)
                            dve.tensor_tensor(G1[:, bass.ds(2 * i + m, 1), :].rearrange("p o (h c) -> p (o h) c", h=2),
                                              pair[2 + m], halves(EB[:, m, :]), ALU.mult).then_inc(tile_free, 1)
            with own.loop(4, 0) as i:
                for j in range(2):
                    ahead("br_att", i, j, 4 * UC if j == 0 else 8 * UC)
                    for m in range(2):
                        tile = 4 * i + (T0["br_att"] + 2 * j + m)
                        if j == 0:
                            scaled(tile, m, EA[:, m, :])
                        else:
                            dve.wait_ge(sig_done, lay * NSIG + 2 * i + (S0N["br_att"] + m + 1))
                            done(tile)
                            dve.tensor_tensor(halves(EA[:, m, :]), pair[2 + m], halves(EB[:, m, :]), ALU.mult)\
                                .then_inc(tile_free, 1)
                            dve.wait_ge(tile_free, lay * NT + tile + 3)
                            k = bass.ds(2 * i + m, 1)
                            dve.tensor_tensor(G1[:, k, :], G1[:, k, :], EA[:, m:m + 1, :], ALU.add).then_inc(val_ready, 1)
                            dve.wait_ge(hi_val, lay * NX + 2 * i + (X0["br_att"] + m + 1))
                            dve.tensor_tensor(ROL[:, k, :], G1[:, k, :], ROH[:, k, :].bitcast(F32),
                                              ALU.subtract).then_inc(x_lo, 1)

            def residual(tile, p, k, gcol, hi, squared):
                done(tile)
                x = XT[:, bass.ds(k, 1), :]
                v = x.rearrange("p o (h c) -> p (o h) c", h=2)
                dve.tensor_tensor(v, v, pair[p], ALU.add).then_inc(tile_free, 1)
                dve.wait_ge(tile_free, lay * NT + tile + 3)
                low_x(bass.ds(k, 1), bass.ds(gcol, 1), hi, squared)

            own.mark(dve.memset(EB[:, 1, :], 0.0))
            own.hold()
            with own.loop(2, 0) as i:
                for j in range(2):
                    ahead("out", i, j)
                    for m in range(2):
                        k = 4 * i + (2 * j + m)
                        residual(k + T0["out"], 2 * j + m, k, 8 * lay + k + 16, lay * NX + k + (X0["out"] + 1),
                                 (2 * lay + 1) * KT + k)

            def gu(i, j):
                ahead("gu", i, j)
                if isinstance(i, int) and i == j == 0:
                    take_rt(2 * lay + 2, (5, 6))
                    dve.wait_ge(rt_taken, 2 * lay + 2)
                tile = 4 * i + (2 * j + T0["gu"])
                f = 2 * i + j
                scaled(tile, 2 * j, EA[:, 0, :])
                dve.wait_ge(sig_done, lay * NSIG + f + (S0N["gu"] + 1))
                own.mark(dve.tensor_tensor(EB[:, 0, :], EB[:, 0, :], EA[:, 0, :], ALU.mult))
                scaled(tile + 1, 2 * j + 1, EA[:, 1, :])
                own.wait()
                dve.wait_ge(tile_free, lay * NT + tile + 4)
                dve.tensor_tensor(EA[:, 1, :], EA[:, 1, :], EB[:, 0, :], ALU.mult).then_inc(val_ready, 1)
                dve.wait_ge(hi_val, lay * NX + f + (X0["gu"] + 1))
                dve.tensor_tensor(AL[:, bass.ds(f, 1), :], EA[:, 1:2, :], AH[:, bass.ds(f, 1), :].bitcast(F32),
                                  ALU.subtract).then_inc(x_lo, 1)

            variance(2 * lay + 2)
            spread_rt(2 * lay + 2)
            gu(0, 0)
            gu(0, 1)
            hold(dve, tile_free, lay * NT + T0["gu"] + 4)
            with own.loop(FT // 2 - 1, 2) as i:
                for j in range(2):
                    gu(i + 1, j)

            def down(i, m):
                k = 2 * i + m
                split(4 * i + (U0["down"] + 2 * m + 1), 1, 11 * P)
                split(4 * i + (U0["down"] + 2 * m + 2), 0, 8 * UC)
                residual(k + T0["down"], m, k, 24 * lay + k + 8, lay * NX + k + (X0["down"] + 1),
                         (2 * lay + 2) * KT + k)

            own.mark(dve.memset(EB[:, 1, :], 0.0))
            own.hold()
            with own.loop(KT // 2, 0) as i:
                for m in range(2):
                    down(i, m)
            assert own.n == LAYER_MARKS, f"marks of a layer: {own.n}"
        own.base, own.n = 0, start + DEPTH * LAYER_MARKS

        dve.wait_ge(x_lo, DEPTH * NX + KT)
        dve.tensor_tensor(XT[:], XT[:], GT[:, 32:40].unsqueeze(2).to_broadcast([P, KT, N]), ALU.mult)\
           .then_inc(xg_ready, 1)
        variance(2 * DEPTH + 1)

    ctx.close()


LAYER_MARKS = 204


def kernel(**inputs):
    import concourse.bacc as bacc
    from concourse.bass_utils import run_bass_kernel_spmd

    nc = bacc.Bacc("TRN2", target_bir_lowering=False, num_devices=1)
    names = ["x_prompt", "x_sample", "cache_k", "cache_v", "state_ret", "page_table", "g_mix", "w_in", "w_br_ret",
             "w_br_att", "w_out", "g_ffn", "w_gu", "w_down", "g_final"]
    data = {n: np.ascontiguousarray(inputs[n]) for n in names}
    data["consts_layer"], data["consts_fixed"] = shape_constants()
    arrays = {f"in_{n}": a for n, a in data.items()}
    args = [nc.dram_tensor(f"in_{n}", a.shape, mybir.dt.from_np(a.dtype), kind="ExternalInput").ap()
            for n, a in data.items()]
    outs = [(1, SEQ, D_MODEL), (DEC_B, DEC_L, D_MODEL), (DEPTH, 1, SEQ, M_HEADS, M_DH), (DEPTH, 1, SEQ, M_HEADS, M_DH),
            (DEPTH, 1, R_HEADS, R_DK, R_DV), (DEPTH, DEC_B, DEC_L, M_HEADS, M_DH),
            (DEPTH, DEC_B, DEC_L, M_HEADS, M_DH), (DEPTH, DEC_B, R_HEADS, R_DK, R_DV)]
    args += [nc.dram_tensor(f"out_{i}", s, F32, kind="ExternalOutput").ap() for i, s in enumerate(outs)]
    build(nc, *args)
    r = run_bass_kernel_spmd(nc, [arrays], core_ids=[0])
    return tuple(r.results[0][f"out_{i}"] for i in range(len(outs)))
```
